# Optimizing a Trainium2 kernel written in Bass

```python
import jax, jax.numpy as jnp
from jax import lax
import numpy as np

D_MODEL = 1024
BATCH = 1
SEQ = 256
DEPTH = 1

CHUNK = 64
EPS = 1e-6

GLA_HEADS = 4
GLA_DK = 64
GLA_DV = 128
GLA_GATE_RANK = 16
GLA_GATE_TAU = 16.0
GLA_GATE_BIAS_INIT = 2.0

ATT_HEADS = 8
ATT_DH = 64
N_BACK_CHUNKS = 8
BAND_CHUNKS = N_BACK_CHUNKS + 1
REL_CLIP = 256
MASK_VALUE = -1e30

N_EXPERTS = 32
TOP_K = 4
D_FF = D_MODEL
SWIGLU_ALPHA = 1.702
SWIGLU_LIMIT = 7.0
MOE_BLOCK = 256

GLA_QK_W = GLA_HEADS * GLA_DK
GLA_V_W = GLA_HEADS * GLA_DV
ATT_W = ATT_HEADS * ATT_DH
MIX_W = GLA_V_W + ATT_W
IN_SIZES = (GLA_QK_W, GLA_QK_W, GLA_V_W, GLA_GATE_RANK, GLA_V_W, ATT_W, ATT_W, ATT_W)
IN_W = sum(IN_SIZES)
IN_SPLITS = [int(s) for s in np.cumsum(IN_SIZES)[:-1]]

kernel_name = "hybrid_gla_bandattn_moe_block"

def rms_norm(x, g):
    xf = x.astype(jnp.float32)
    y = xf * lax.rsqrt(jnp.mean(xf * xf, axis=-1, keepdims=True) + EPS)
    return (y * g.astype(jnp.float32)).astype(x.dtype)

def gla_mixer(q, k, v, gate_lr, g_out, gate_up, gate_bias, norm_g):
    B, S = q.shape[0], q.shape[1]
    NC = S // CHUNK
    f32 = jnp.float32
    qc = q.astype(f32).reshape(B, NC, CHUNK, GLA_HEADS, GLA_DK) * (GLA_DK ** -0.5)
    kc = k.astype(f32).reshape(B, NC, CHUNK, GLA_HEADS, GLA_DK)
    vc = v.astype(f32).reshape(B, NC, CHUNK, GLA_HEADS, GLA_DV)
    log_a = jax.nn.log_sigmoid((gate_lr @ gate_up + gate_bias).astype(f32)) / GLA_GATE_TAU
    log_a = log_a.reshape(B, NC, CHUNK, GLA_HEADS, GLA_DK)
    cum = jnp.cumsum(log_a, axis=2)
    tot = cum[:, :, -1]
    k_dec = kc * jnp.exp(tot[:, :, None] - cum)
    u = jnp.einsum('bnchk,bnchv->bnhkv', k_dec, vc)

    def step(state, inp):
        decay, u_n = inp
        state = decay[..., None] * state + u_n
        return state, state

    s0 = jnp.zeros((B, GLA_HEADS, GLA_DK, GLA_DV), f32)
    _, states = lax.scan(step, s0, (jnp.moveaxis(jnp.exp(tot), 1, 0), jnp.moveaxis(u, 1, 0)))
    states = jnp.moveaxis(states, 0, 1)
    o = jnp.einsum('bnchk,bnhkv->bnchv', qc, states)
    o = rms_norm(o, norm_g).reshape(B, S, GLA_V_W)
    o = o * jax.nn.silu(g_out.astype(f32))
    return o.astype(q.dtype)

def band_chunk_attention(q, k, v, q_norm_g, k_norm_g, rel_bias):
    B, S = q.shape[0], q.shape[1]
    NC = S // CHUNK
    qn = rms_norm(q.reshape(B, S, ATT_HEADS, ATT_DH), q_norm_g).reshape(B, NC, CHUNK, ATT_HEADS, ATT_DH)
    kn = rms_norm(k.reshape(B, S, ATT_HEADS, ATT_DH), k_norm_g).reshape(B, NC, CHUNK, ATT_HEADS, ATT_DH)
    vc = v.reshape(B, NC, CHUNK, ATT_HEADS, ATT_DH)

    def band(t):
        tp = jnp.pad(t, ((0, 0), (N_BACK_CHUNKS, 0), (0, 0), (0, 0), (0, 0)))
        tb = jnp.stack([tp[:, i:i + NC] for i in range(BAND_CHUNKS)], axis=2)
        return tb.reshape(B, NC, BAND_CHUNKS * CHUNK, ATT_HEADS, ATT_DH)

    kb, vb = band(kn), band(vc)
    scores = jnp.einsum('bnqhd,bnkhd->bnhqk', qn, kb).astype(jnp.float32) * (ATT_DH ** -0.5)
    rel = (N_BACK_CHUNKS * CHUNK + np.arange(CHUNK)[:, None]) - np.arange(BAND_CHUNKS * CHUNK)[None, :]
    idx = np.clip(rel, -REL_CLIP, REL_CLIP) + REL_CLIP
    bias = rel_bias[:, idx].astype(jnp.float32)
    key_chunk = np.arange(NC)[:, None] - N_BACK_CHUNKS + np.arange(BAND_CHUNKS)[None, :]
    valid = np.repeat(key_chunk >= 0, CHUNK, axis=1)
    scores = jnp.where(valid[None, :, None, None, :], scores + bias[None, None], MASK_VALUE)
    p = jax.nn.softmax(scores, axis=-1).astype(vb.dtype)
    o = jnp.einsum('bnhqk,bnkhd->bnqhd', p, vb)
    return o.reshape(B, S, ATT_W)

def moe_ffn(h, router_w, router_b, w_in, b_in, w_out, b_out):
    N, D = h.shape
    logits = (h @ router_w + router_b).astype(jnp.float32)
    top_val, top_idx = lax.top_k(logits, TOP_K)
    gates = jax.nn.softmax(top_val, axis=-1).astype(h.dtype)

    A = N * TOP_K
    n_blocks = -(-A // MOE_BLOCK) + N_EXPERTS
    P = n_blocks * MOE_BLOCK
    flat_e = top_idx.reshape(-1).astype(jnp.int32)
    flat_tok = jnp.repeat(jnp.arange(N, dtype=jnp.int32), TOP_K)
    flat_g = gates.reshape(-1)
    order = jnp.argsort(flat_e, stable=True)
    e_sorted, tok_sorted, g_sorted = flat_e[order], flat_tok[order], flat_g[order]
    counts = jnp.bincount(flat_e, length=N_EXPERTS).astype(jnp.int32)
    start = jnp.cumsum(counts) - counts
    padded = ((counts + MOE_BLOCK - 1) // MOE_BLOCK) * MOE_BLOCK
    pend = jnp.cumsum(padded)
    pstart = pend - padded
    dest = pstart[e_sorted] + (jnp.arange(A, dtype=jnp.int32) - start[e_sorted])
    buf_tok = jnp.full((P,), N, jnp.int32).at[dest].set(tok_sorted)
    buf_g = jnp.zeros((P,), h.dtype).at[dest].set(g_sorted)
    block_expert = jnp.minimum(
        jnp.searchsorted(pend, jnp.arange(n_blocks, dtype=jnp.int32) * MOE_BLOCK, side='right'),
        N_EXPERTS - 1).astype(jnp.int32)
    h_pad = jnp.concatenate([h, jnp.zeros((1, D), h.dtype)], axis=0)
    xb = h_pad[buf_tok].reshape(n_blocks, MOE_BLOCK, D)

    def expert_block(args):
        xblk, e = args
        hc = xblk @ w_in[e] + b_in[e]
        glu, lin = hc[:, :D_FF], hc[:, D_FF:]
        glu = jnp.minimum(glu, SWIGLU_LIMIT)
        lin = jnp.clip(lin, -SWIGLU_LIMIT, SWIGLU_LIMIT)
        act = glu * jax.nn.sigmoid(SWIGLU_ALPHA * glu) * (lin + 1.0)
        return act @ w_out[e] + b_out[e]

    y = lax.map(expert_block, (xb, block_expert)).reshape(P, D)
    out = jnp.zeros((N + 1, D), h.dtype).at[buf_tok].add(y * buf_g[:, None])
    return out[:N]

def hybrid_layer(x, norm1_g, w_in, gla_gate_up, gla_gate_bias, gla_norm_g, q_norm_g, k_norm_g,
                 rel_bias, w_out, norm2_g, router_w, router_b, moe_w_in, moe_b_in, moe_w_out, moe_b_out):
    B, S, D = x.shape
    h = rms_norm(x, norm1_g)
    proj = h @ w_in
    g_q, g_k, g_v, g_lr, g_og, a_q, a_k, a_v = jnp.split(proj, IN_SPLITS, axis=-1)
    o_gla = gla_mixer(g_q, g_k, g_v, g_lr, g_og, gla_gate_up, gla_gate_bias, gla_norm_g)
    o_att = band_chunk_attention(a_q, a_k, a_v, q_norm_g, k_norm_g, rel_bias)
    x = x + jnp.concatenate([o_gla, o_att], axis=-1) @ w_out
    h2 = rms_norm(x, norm2_g).reshape(B * S, D)
    y = moe_ffn(h2, router_w, router_b, moe_w_in, moe_b_in, moe_w_out, moe_b_out)
    return x + y.reshape(B, S, D)

def setup_inputs(seed: int = 0) -> dict:
    key = jax.random.key(seed)
    ks = jax.random.split(key, 17)
    f32 = jnp.float32
    L, D = DEPTH, D_MODEL
    nrm = lambda k, shape, s: jax.random.normal(k, shape, f32) * s
    return {
        "x": nrm(ks[0], (BATCH, SEQ, D), 1.0),
        "norm1_g": 1.0 + nrm(ks[1], (L, D), 0.02),
        "w_in": nrm(ks[2], (L, D, IN_W), D ** -0.5),
        "gla_gate_up": nrm(ks[3], (L, GLA_GATE_RANK, GLA_QK_W), GLA_GATE_RANK ** -0.5),
        "gla_gate_bias": GLA_GATE_BIAS_INIT + nrm(ks[4], (L, GLA_QK_W), 0.1),
        "gla_norm_g": 1.0 + nrm(ks[5], (L, GLA_DV), 0.02),
        "q_norm_g": 1.0 + nrm(ks[6], (L, ATT_DH), 0.02),
        "k_norm_g": 1.0 + nrm(ks[7], (L, ATT_DH), 0.02),
        "rel_bias": nrm(ks[8], (L, ATT_HEADS, 2 * REL_CLIP + 1), 0.3),
        "w_out": nrm(ks[9], (L, MIX_W, D), MIX_W ** -0.5),
        "norm2_g": 1.0 + nrm(ks[10], (L, D), 0.02),
        "router_w": nrm(ks[11], (L, D, N_EXPERTS), D ** -0.5),
        "router_b": nrm(ks[12], (L, N_EXPERTS), 0.01),
        "moe_w_in": nrm(ks[13], (L, N_EXPERTS, D, 2 * D_FF), D ** -0.5),
        "moe_b_in": nrm(ks[14], (L, N_EXPERTS, 2 * D_FF), 0.01),
        "moe_w_out": nrm(ks[15], (L, N_EXPERTS, D_FF, D), D_FF ** -0.5),
        "moe_b_out": nrm(ks[16], (L, N_EXPERTS, D), 0.01),
    }

def reference(x, norm1_g, w_in, gla_gate_up, gla_gate_bias, gla_norm_g, q_norm_g, k_norm_g,
              rel_bias, w_out, norm2_g, router_w, router_b, moe_w_in, moe_b_in, moe_w_out, moe_b_out):
    for l in range(DEPTH):
        x = hybrid_layer(x, norm1_g[l], w_in[l], gla_gate_up[l], gla_gate_bias[l], gla_norm_g[l],
                         q_norm_g[l], k_norm_g[l], rel_bias[l], w_out[l], norm2_g[l], router_w[l],
                         router_b[l], moe_w_in[l], moe_b_in[l], moe_w_out[l], moe_b_out[l])
    return x


_drawn_inputs = setup_inputs


def setup_inputs(seed=0):
    import zlib

    import numpy as np

    out = dict(_drawn_inputs(seed))
    spreads = {}
    factors = {'q_norm_g': 3.012,
     'k_norm_g': 8.0,
     'moe_b_in': 8.0,
     'moe_b_out': 8.0,
     'gla_norm_g': 2.912,
     'router_b': 2.815}
    for name, (base, spread) in spreads.items():
        noise = np.random.default_rng([zlib.crc32(name.encode()), seed]).standard_normal(out[name].shape)
        drawn = base * np.exp(spread * noise) if base else spread * noise
        out[name] = __import__('jax').numpy.asarray(drawn.astype(out[name].dtype))
    for name, factor in factors.items():
        out[name] = (out[name] * factor).astype(out[name].dtype)
    return out
```

```python
from contextlib import ExitStack

import concourse.bass as bass
from concourse import mybir

P = 128
D = 1024
S = 256
T = S // P
CHUNK = 64
NCH = S // CHUNK
KD = D // P
EPS = 1e-6
GH, GDK, GDV, GRANK, GTAU = 4, 64, 128, 16, 16.0
AH, ADH = 8, 64
REL_CLIP = 256
MASK_VALUE = -1e30
NE, TOPK, F = 32, 4, 1024
ALPHA, LIMIT = 1.702, 7.0
GROUP = 512
AQ, AK, AV, GQK, GV, OG = range(6)
GROUP_COL = (1552, 2064, 2576, 0, 512, 1040)
LR_COL = 1024

SLOTS = 64
ROUNDS = S // SLOTS
PAIRS = 2
EPI = 2 * PAIRS
ITERS = NE // EPI
CHUNK_F = 2048
RING = 16
JOB_CHUNKS = 2 * KD + KD
ITER_CHUNKS = PAIRS * JOB_CHUNKS
GATE_TILE = RING - 4

F32 = mybir.dt.float32
BF16 = mybir.dt.bfloat16
I32 = mybir.dt.int32
U32 = mybir.dt.uint32
ALU = mybir.AluOpType
ACT = mybir.ActivationFunctionType
AX = mybir.AxisListType.X


def build(nc, x, norm1_g, w_in, gla_gate_up, gla_gate_bias, gla_norm_g, q_norm_g, k_norm_g,
          rel_bias, w_out, norm2_g, router_w, router_b, moe_w_in, moe_b_in, moe_w_out,
          moe_b_out, out):
    with ExitStack() as ctx:
        def sb(name, shape, dt=F32):
            return ctx.enter_context(nc.sbuf_tensor(name, shape, dt))

        def sem(name):
            return ctx.enter_context(nc.semaphore(name))

        ring = sb("ring", [P, RING, CHUNK_F])
        acc = sb("acc", [P, T, D])
        area = sb("area", [P, 14592])
        bias_parts = sb("bias_parts", [P, 3 * D], BF16)
        ident = sb("ident", [P, P])
        later = sb("later", [P, P])
        before = sb("before", [P, P])
        ones = sb("ones", [P, P])
        chunk_of = sb("chunk_of", [P, 2])
        eps = sb("eps", [P, 1])
        slot_iota = sb("slot_iota", [P, SLOTS])
        expert_iota = sb("expert_iota", [P, NE])
        expert_diff = sb("expert_diff", [P, P])
        pair_first = sb("pair_first", [P, NE // 2])
        params = sb("params", [P, P])
        gains = sb("gains", [P, 19])
        w_lr = sb("w_lr", [P, KD, GRANK])
        w_router = sb("w_router", [P, KD, NE])
        gate_up = sb("gate_up", [GRANK + 1, S])
        b_router = sb("b_router", [P, NE])
        stat = sb("stat", [P, 128])
        gates = sb("gates", [P, T, NE])
        mask = sb("mask", [P, T, NE])
        slot_of = sb("slot_of", [P, T, ROUNDS, NE])
        top_val = sb("top_val", [P, T, 8])
        top_idx = sb("top_idx", [P, T, 8], U32)
        top_idx_f = sb("top_idx_f", [P, T, 8])
        top_exp = sb("top_exp", [P, T, TOPK])
        counts = sb("counts", [1, 64])
        flags = sb("flags", [1, 32], I32)

        def part(base, off, *dims):
            n = 1
            for d in dims:
                n *= d
            v = base[:, off:off + n]
            if len(dims) == 1:
                return v
            names = "abc"[:len(dims)]
            return v.rearrange("p (%s) -> p %s" % (" ".join(names), " ".join(names)),
                               **{c: d for c, d in zip(names, dims)})

        hT = part(area, 0, KD, S)
        mixT = hT
        proj = part(area, 2048, T, 6 * GROUP)
        xn = part(area, 2048, T, D)
        o = 8192
        gla_qT = part(area, o, 2, S)
        log_a = part(area, o + 512, T, S)
        decay_tok = part(area, o + 1024, T, S)
        k_dec = part(area, o + 1536, T, S)
        state = part(area, o + 2048, NCH, 2, S)
        gla_o = part(area, o + 4096, T, GROUP)
        out_gate = part(area, o + 5120, T, GROUP)
        lrT = part(area, o + 6144, S)
        spare = ring[:, :, :].rearrange("p s f -> p (s f)")
        A0 = 6 * CHUNK_F
        scores = [part(spare, A0, AH, P), part(spare, A0 + 1024, AH, S)]
        probT = [part(spare, A0 + 3072, AH, S), part(spare, A0 + 5120, AH, P)]
        rel = [part(spare, A0 + 6144, AH, P), part(spare, A0 + 7168, AH, S)]
        att_qT = part(spare, A0 + 9216, AH // 2, S)
        att_kT = part(spare, A0 + 10240, AH // 2, S)
        square = part(spare, A0 + 11264, 2 * GROUP)
        bias_raw = part(spare, 3 * CHUNK_F, 3 * D)
        bias_rest = part(spare, 3 * CHUNK_F + 3 * D, 3 * D)
        w_buf = [part(spare, (GATE_TILE + 2 * b) * CHUNK_F, KD, GROUP) for b in range(2)]
        w_out_sb = part(spare, GATE_TILE * CHUNK_F, KD, D)
        xn2 = part(area, 0, T, D)
        squares2 = part(area, 5120, T, D)
        h2T = part(area, 2048, KD, S)
        glu_c = part(area, 0, 2, GROUP)
        sig = part(area, 1024, 2, GROUP)
        lin_c = part(area, 2048, 2, GROUP)
        act_t = part(area, 3072, 2, GROUP)
        h2_parts = [part(area, 4096 + 1024 * i, 1024).bitcast(BF16).rearrange("p (t d) -> p t d", t=T)
                    for i in range(3)]
        xeT = [part(area, 7168 + 1024 * i, KD, P) for i in range(PAIRS)]
        actT = part(area, 9216, KD, P)
        y_sb = part(area, 10240, 2, GROUP)
        gatherT = part(area, 11264, S)
        pick = [part(area, 11520 + 128 * i, 128).bitcast(BF16).rearrange("p (t s) -> p t s", t=T)
                for i in range(PAIRS)]
        pick_gated = [part(area, 11776 + 256 * i, T, P) for i in range(PAIRS)]
        bias_pick = [part(area, 12288 + 64 * i, 64).bitcast(BF16) for i in range(PAIRS)]
        onehot = part(area, 12416, T * TOPK, NE)
        gated_hot = part(area, 12672, T * TOPK, NE)
        rest = part(area, 12928, D)

        bank = [ctx.enter_context(nc.psum_tensor(f"bank{i}", [P, 512], F32)) for i in range(8)]

        x_in, params_in, small_in, rel_in, bias_in = map(sem, ("x_in", "params_in", "small_in", "rel_in", "bias_in"))
        w_in_full = [sem(f"w_in_full{g}") for g in range(6)]
        w_out_full = [sem(f"w_out_full{b}") for b in range(2)]
        ring_full = [sem(f"ring_full{s}") for s in range(RING)]
        result_ready = sem("result_ready")
        pool_step, ident_ready, consts_ready, bias_split = map(sem, ("pool_step", "ident_ready", "consts_ready", "bias_split"))
        vec_step, act_step = sem("vec_step"), sem("act_step")
        sq1, rstd1, xn_ready = map(sem, ("sq1", "rstd1", "xn_ready"))
        params_turned, gains_ready = map(sem, ("params_turned", "gains_ready"))
        hT_psum, hT_ready = map(sem, ("hT_psum", "hT_ready"))
        proj_psum, proj_ready = map(sem, ("proj_psum", "proj_ready"))
        lr_psum, lr_ready, z_psum, abs_z, log_ready = map(sem, ("lr_psum", "lr_ready", "z_psum", "abs_z", "log_ready"))
        qk_squared, qk_summed, qk_root, qk_normed = map(sem, ("qk_squared", "qk_summed", "qk_root", "qk_normed"))
        qkT_psum, qkT_ready = map(sem, ("qkT_psum", "qkT_ready"))
        score_psum, score_ready, max_ready, exp_ready, prob_ready = map(
            sem, ("score_psum", "score_ready", "max_ready", "exp_ready", "prob_ready"))
        glaq_psum, glaq_ready = map(sem, ("glaq_psum", "glaq_ready"))
        rev_psum, rev_exp, kdec_ready = map(sem, ("rev_psum", "rev_exp", "kdec_ready"))
        probT_psum, probT_ready = map(sem, ("probT_psum", "probT_ready"))
        u_psum, state_ready = map(sem, ("u_psum", "state_ready"))
        att_psum, att_ready = map(sem, ("att_psum", "att_ready"))
        gate_sig, gla_psum, gla_squared, gla_summed, gla_root, gla_normed = map(
            sem, ("gate_sig", "gla_psum", "gla_squared", "gla_summed", "gla_root", "gla_normed"))
        glaT_psum, glaT_ready = map(sem, ("glaT_psum", "glaT_ready"))
        mix_psum, x1_ready, sq2, rstd2, xn2_ready = map(
            sem, ("mix_psum", "x1_ready", "sq2", "rstd2", "xn2_ready"))
        h2T_psum, h2T_ready, parts_ready, logit_psum, top_ready, top_expd = map(
            sem, ("h2T_psum", "h2T_ready", "parts_ready", "logit_psum", "top_ready", "top_expd"))
        mask_ready, rank_psum, slots_ready, flags_ready = map(
            sem, ("mask_ready", "rank_psum", "slots_ready", "flags_ready"))
        chunks_used, route_ready, pack_psum, pack_ready, hidden_psum = map(
            sem, ("chunks_used", "route_ready", "pack_psum", "pack_ready", "hidden_psum"))
        glu_clipped, lin_clipped, sig_ready, glu_ready, hidden_ready = map(
            sem, ("glu_clipped", "lin_clipped", "sig_ready", "glu_ready", "hidden_ready"))
        hiddenT_psum, hiddenT_ready, gatherT_psum, gatherT_ready = map(
            sem, ("hiddenT_psum", "hiddenT_ready", "gatherT_psum", "gatherT_ready"))
        y_psum, y_ready, comb_psum, comb_added = map(sem, ("y_psum", "y_ready", "comb_psum", "comb_added"))

        G1, G2, GN, GQ, GK = 0, KD, 2 * KD, 2 * KD + 1, 2 * KD + 2
        block = ctx.enter_context(nc.Block())

        def flag_column(quad, rnd):
            return (rnd - 1) * ITERS + quad

        def all_rounds(eng, run):
            run(0, 0, 0)
            with eng.Fori(1, ITERS) as it:
                run(it, it, 0)
            eng.wait_ge(flags_ready, 1)
            with eng.If(eng.value_load(flags[0:1, 24:25], min_val=0, max_val=1) != 0):
                done = eng.alloc_register("iterations_done")
                eng.reg_mov(done, ITERS)
                for rnd in range(1, ROUNDS):
                    with eng.Fori(0, ITERS) as quad:
                        col = eng.snap(quad + (rnd - 1) * ITERS)
                        flag = eng.value_load(flags[0:1, bass.ds(col, 1)], min_val=0, max_val=1)
                        with eng.If(flag != 0):
                            it = eng.snap(done, min_val=ITERS, max_val=ITERS * ROUNDS)
                            run(it, quad, rnd)
                            eng.reg_add(done, done, 1)
                        with eng.Else():
                            eng.nop()
                        eng.nop()
            with eng.Else():
                eng.nop()
            eng.nop()

        @block.sync
        def _(sp):
            sp.dma_start(acc[:, :, :], x[0].rearrange("(t p) d -> p t d", p=P)).then_inc(x_in, 16)

            def load_group(g):
                c = GROUP_COL[g]
                sp.dma_start(w_buf[g % 2], w_in[0, :, c:c + GROUP].rearrange("(k p) n -> p k n", p=P))\
                    .then_inc(w_in_full[g], 16)

            def fill(slot, quad, c):
                job, r = divmod(c, JOB_CHUNKS)
                if r < 2 * KD:
                    k, e = divmod(r, 2)
                    src = moe_w_in[0, bass.ds(quad * EPI + 2 * job + e, 1), k * P:(k + 1) * P, :]
                    dst = ring[:, slot, :].rearrange("p (a f) -> p a f", a=1)
                    src = src.rearrange("a p f -> p a f")
                else:
                    k, e = divmod(r - 2 * KD, 2)
                    src = moe_w_out[0, bass.ds(quad * EPI + 2 * job + e, 1), 2 * k * P:2 * (k + 1) * P, :]
                    src = src.rearrange("a (k p) d -> p (a k) d", p=P)
                    dst = ring[:, slot, :].rearrange("p (k d) -> p k d", k=2)
                sp.dma_start(dst, src).then_inc(ring_full[slot], 16)

            load_group(0)
            load_group(1)
            sp.wait_ge(proj_psum, 2)
            load_group(2)
            for c in range(3):
                fill(c, 0, c)
            sp.wait_ge(bias_split, 1)
            for g in range(3, 6):
                sp.wait_ge(proj_psum, 2 * (g - 1))
                load_group(g)
                fill(g, 0, g)
            for b in range(2):
                sp.wait_ge(proj_psum, 2 * (5 + b))
                sp.dma_start(w_out_sb[:, 4 * b:4 * b + 4, :],
                             w_out[0, b * 512:(b + 1) * 512, :].rearrange("(k p) n -> p k n", p=P))\
                    .then_inc(w_out_full[b], 16)
            sp.wait_ge(gla_summed, 2)
            sp.wait_ge(att_psum, 2)
            for c in range(6, GATE_TILE):
                fill(c, 0, c)
            sp.wait_ge(mix_psum, 4)
            for c in range(GATE_TILE, RING):
                fill(c, 0, c)

            def run(it, quad, rnd):
                first = isinstance(it, int)
                for c in range(RING if first else 0, ITER_CHUNKS):
                    sp.wait_ge(chunks_used, it * ITER_CHUNKS + c - RING + 1)
                    fill(c % RING, quad, c)

            all_rounds(sp, run)
            sp.wait_ge(result_ready, 1)
            sp.dma_start(out[0].rearrange("(t p) d -> p t d", p=P), acc[:, :, :]).then_inc(x_in, 16)
            sp.wait_ge(x_in, 32)

        @block.gpsimd
        def _(pool):
            steps = [0]

            def step(ins):
                steps[0] += 1
                ins.then_inc(pool_step, 1)
                pool.wait_ge(pool_step, steps[0])

            step(pool.memset(ident[:, :], 0.0))
            step(pool.memset(eps[:, :], EPS))
            pool.affine_select(out=ident[:, :], in_=ident[:, :], compare_op=ALU.not_equal, fill=1.0,
                               base=0, pattern=[[-1, P]], channel_multiplier=1).then_inc(ident_ready, 1)
            pool.wait_ge(ident_ready, 1)
            step(pool.memset(ones[:, :], 1.0))
            step(pool.memset(lrT[0:32, :], 1.0))
            step(pool.memset(chunk_of[:, :], 0.0))
            step(pool.memset(state[:, :, :, :], 0.0))
            step(pool.memset(chunk_of[0:64, 0:1], 1.0))
            step(pool.memset(chunk_of[64:128, 1:2], 1.0))
            step(pool.affine_select(out=later[:, :], in_=ones[:, :], compare_op=ALU.is_gt, fill=0.0,
                                    base=0, pattern=[[-1, P]], channel_multiplier=1))
            step(pool.affine_select(out=before[:, :], in_=ones[:, :], compare_op=ALU.is_gt, fill=0.0,
                                    base=0, pattern=[[1, P]], channel_multiplier=-1))
            step(pool.memset(later[64:128, 0:64], 0.0))
            step(pool.iota(slot_iota[:, :], [[1, SLOTS]], base=0, channel_multiplier=0,
                           allow_small_or_imprecise_dtypes=True))
            step(pool.iota(expert_iota[:, :], [[1, NE]], base=0, channel_multiplier=0,
                           allow_small_or_imprecise_dtypes=True))
            step(pool.iota(pair_first[:, :], [[2, NE // 2]], base=0, channel_multiplier=0,
                           allow_small_or_imprecise_dtypes=True))
            for i in range(3):
                step(pool.iota(expert_diff[32 * i:32 * i + 32, :], [[-1, 2], [0, 64]], base=0,
                               channel_multiplier=1, allow_small_or_imprecise_dtypes=True))
            step(pool.memset(expert_diff[96:128, :], -5.0))
            pool.memset(bias_parts[96:128, :], 0.0).then_inc(consts_ready, 1)
            pool.wait_ge(consts_ready, 1)
            pool.wait_ge(bias_in, 96)
            step(pool.tensor_copy(bias_parts[0:96, :], bias_raw[0:96, :]))
            step(pool.tensor_tensor(bias_rest[0:96, :], bias_raw[0:96, :], bias_parts[0:96, :], ALU.subtract))
            step(pool.tensor_copy(bias_parts[32:64, :], bias_rest[32:64, :]))
            step(pool.tensor_copy(bias_parts[64:96, :], bias_rest[64:96, :]))
            step(pool.tensor_tensor(bias_rest[64:96, :], bias_rest[64:96, :], bias_parts[64:96, :], ALU.subtract))
            pool.tensor_copy(bias_parts[64:96, :], bias_rest[64:96, :]).then_inc(bias_split, 1)

        @block.scalar
        def _(act):
            act.dma_start(params[0:8, :], norm1_g[0].rearrange("(k p) -> k p", p=P)).then_inc(params_in, 16)
            act.dma_start(params[8:16, :], norm2_g[0].rearrange("(k p) -> k p", p=P)).then_inc(params_in, 16)
            act.dma_start(params[16:17, :], gla_norm_g).then_inc(params_in, 16)
            for row, g in ((17, q_norm_g), (18, k_norm_g)):
                for b in range(2):
                    act.dma_start(params[row:row + 1, b * 64:b * 64 + 64], g).then_inc(params_in, 16)
            act.dma_start(w_lr[:, :, :], w_in[0, :, LR_COL:LR_COL + GRANK].rearrange("(k p) n -> p k n", p=P))\
                .then_inc(small_in, 16)
            act.dma_start(gate_up[0:GRANK, :], gla_gate_up[0]).then_inc(small_in, 16)
            act.dma_start(gate_up[GRANK:GRANK + 1, :], gla_gate_bias).then_inc(small_in, 16)
            act.dma_start(w_router[:, :, :], router_w[0].rearrange("(k p) n -> p k n", p=P)).then_inc(small_in, 16)
            act.dma_start(b_router[:, :], bass.AP(router_b.tensor, router_b.offset, [[0, P], [1, NE]]))\
                .then_inc(small_in, 16)
            for t in range(T):
                keys = P * (t + 1)
                off = REL_CLIP + P * t - (keys - 1)
                act.dma_start(rel[t], bass.AP(rel_bias.tensor, rel_bias.offset + off,
                                              [[1, P], [2 * REL_CLIP + 1, AH], [1, keys]])).then_inc(rel_in, 16)
            for i in range(3):
                act.dma_start(bias_raw[32 * i:32 * i + 32, 0:2 * D], moe_b_in[0]).then_inc(bias_in, 16)
                act.dma_start(bias_raw[32 * i:32 * i + 32, 2 * D:3 * D], moe_b_out[0]).then_inc(bias_in, 16)

            act.wait_ge(x_in, 16)
            act.wait_ge(ident_ready, 1)
            for t in range(T):
                act.activation(hT[:, 4 * t:4 * t + 4, :], acc[:, t, :].rearrange("p (a b) -> p a b", a=4),
                               ACT.Square, accum_out=stat[:, t:t + 1]).then_inc(sq1, 1)
            act.wait_ge(sq1, 2)
            act.activation(stat[:, 2:4], stat[:, 0:2], ACT.Sqrt, bias=eps[:, 0:1], scale=1.0 / D).then_inc(rstd1, 1)

            def project_out(g):
                for t in range(T):
                    act.wait_ge(proj_psum, 2 * g + t + 1)
                    act.activation(proj[:, t, g * GROUP:(g + 1) * GROUP], bank[4 + 2 * (g % 2) + t][:, :],
                                   ACT.Copy).then_inc(proj_ready, 1)

            def squares(g):
                act.wait_ge(proj_ready, 2 * g + 2)
                if g:
                    act.wait_ge(qk_summed, 2 * g)
                for t in range(T):
                    act.activation(square[:, t * GROUP:(t + 1) * GROUP], proj[:, t, g * GROUP:(g + 1) * GROUP],
                                   ACT.Square).then_inc(qk_squared, 1)
                act.wait_ge(qk_summed, 2 * g + 2)
                act.activation(stat[:, 32 + 16 * g:48 + 16 * g], stat[:, 64 + 16 * g:80 + 16 * g], ACT.Sqrt,
                               bias=eps[:, 0:1], scale=1.0 / ADH).then_inc(qk_root, 1)

            project_out(AQ)
            squares(0)
            project_out(AK)
            squares(1)
            act.wait_ge(lr_psum, 1)
            act.wait_ge(consts_ready, 1)
            act.activation(lrT[0:GRANK, :], bank[0][0:GRANK, 0:S], ACT.Copy).then_inc(lr_ready, 1)
            project_out(AV)
            for n in range(4):
                act.wait_ge(qkT_psum, n + 1)
                dst = (att_qT, att_kT)[n // 2]
                gain = (GQ, GK)[n // 2]
                act.activation(dst[:, 2 * (n % 2):2 * (n % 2) + 2, :],
                               bank[n][:, :].rearrange("p (a b) -> p a b", a=2), ACT.Copy,
                               scale=gains[:, gain:gain + 1]).then_inc(qkT_ready, 1)
            project_out(GQK)
            act.wait_ge(glaq_psum, 1)
            act.activation(gla_qT, bank[3][:, :].rearrange("p (a b) -> p a b", a=2), ACT.Copy,
                           scale=GDK ** -0.5).then_inc(glaq_ready, 1)

            def exps(t):
                act.wait_ge(max_ready, t + 1)
                for h in range(AH):
                    ins = act.activation(scores[t][:, h, :], scores[t][:, h, :], ACT.Exp,
                                         bias=stat[:, 8 + 8 * t + h:9 + 8 * t + h],
                                         accum_out=stat[:, 96 + 8 * t + h:97 + 8 * t + h])
                ins.then_inc(exp_ready, 1)

            exps(0)
            act.wait_ge(z_psum, 1)
            z = bank[2][:, :].rearrange("p (t n) -> p t n", t=T)
            act.activation(decay_tok, z, ACT.Abs).then_inc(abs_z, 1)
            act.wait_ge(abs_z, 1)
            act.activation(k_dec, decay_tok, ACT.Exp, scale=-1.0).then_inc(abs_z, 1)
            act.wait_ge(abs_z, 2)
            act.wait_ge(consts_ready, 1)
            act.activation(decay_tok, k_dec, ACT.Ln, bias=ones[:, 0:1]).then_inc(abs_z, 1)
            project_out(GV)
            exps(1)
            project_out(OG)
            act.wait_ge(rev_psum, 2)
            act.activation(decay_tok, bank[4][:, :].rearrange("p (t n) -> p t n", t=T), ACT.Exp,
                           scale=1.0 / GTAU).then_inc(rev_exp, 1)
            act.activation(stat[:, 24:32], bank[5][:, 0:8], ACT.Exp, scale=1.0 / GTAU).then_inc(rev_exp, 1)
            act.wait_ge(proj_ready, 12)
            act.activation(out_gate, proj[:, :, 5 * GROUP:6 * GROUP], ACT.Sigmoid).then_inc(gate_sig, 1)
            for n in range(2):
                act.wait_ge(probT_psum, n + 1)
                act.activation(probT[0][:, 4 * n:4 * n + 4, 0:P],
                               bank[n][:, :].rearrange("p (a b) -> p a b", a=4), ACT.Copy).then_inc(probT_ready, 1)
            for n in range(4):
                act.wait_ge(probT_psum, n + 3)
                dst = probT[0][:, 4 * n:4 * n + 4, P:S] if n < 2 else probT[1][:, 4 * (n - 2):4 * (n - 2) + 4, :]
                act.activation(dst, bank[(0, 1, 4, 5)[n]][:, :].rearrange("p (a b) -> p a b", a=4), ACT.Copy)\
                    .then_inc(probT_ready, 1)
            for t in range(T):
                act.wait_ge(gla_psum, t + 1)
                act.activation(square[:, t * GROUP:(t + 1) * GROUP], bank[2 + t][:, :], ACT.Square)\
                    .then_inc(gla_squared, 1)
            act.wait_ge(gla_summed, 2)
            act.activation(stat[:, 120:128], stat[:, 112:120], ACT.Sqrt, bias=eps[:, 0:1], scale=1.0 / GDV)\
                .then_inc(gla_root, 1)
            for n in range(2):
                act.wait_ge(att_psum, n + 1)
                act.activation(mixT[:, 4 + 2 * n:6 + 2 * n, :], bank[n][:, :].rearrange("p (a b) -> p a b", a=2),
                               ACT.Copy).then_inc(att_ready, 1)
            for n in range(2):
                act.wait_ge(glaT_psum, n + 1)
                act.activation(mixT[:, 2 * n:2 * n + 2, :], bank[4 + n][:, :].rearrange("p (a b) -> p a b", a=2),
                               ACT.Copy, scale=gains[:, GN:GN + 1]).then_inc(glaT_ready, 1)
            for t in range(T):
                act.wait_ge(x1_ready, 2 * t + 2)
                act.activation(squares2[:, t, :], acc[:, t, :], ACT.Square, accum_out=stat[:, t:t + 1]).then_inc(sq2, 1)
            act.wait_ge(sq2, 2)
            act.activation(stat[:, 2:4], stat[:, 0:2], ACT.Sqrt, bias=eps[:, 0:1], scale=1.0 / D).then_inc(rstd2, 1)
            for k in range(KD):
                act.wait_ge(h2T_psum, k // 2 + 1)
                act.activation(h2T[:, k, :], bank[2 + k // 2][:, (k % 2) * S:(k % 2) * S + S], ACT.Copy,
                               scale=gains[:, G2 + k:G2 + k + 1]).then_inc(h2T_ready, 1)
            act.wait_ge(top_ready, 1)
            for t in range(T):
                act.activation(top_exp[:, t, :], top_val[:, t, 0:TOPK], ACT.Exp, bias=stat[:, 4 + t:5 + t])\
                    .then_inc(top_expd, 1)

            def run(it, quad, rnd):
                for a in range(PAIRS):
                    j = it * PAIRS + a
                    for hf in range(2):
                        act.wait_ge(glu_clipped, 2 * j + hf + 1)
                        act.activation(sig[:, hf, :], glu_c[:, hf, :], ACT.Sigmoid, scale=ALPHA)\
                            .then_inc(sig_ready, 1)
                    for hf in range(2):
                        act.wait_ge(hiddenT_psum, 2 * j + hf + 1)
                        act.activation(actT[:, 4 * hf:4 * hf + 4, :],
                                       bank[4 + hf][:, :].rearrange("p (a b) -> p a b", a=4), ACT.Copy)\
                            .then_inc(hiddenT_ready, 1)
                    act.wait_ge(gatherT_psum, j + 1)
                    act.activation(gatherT, bank[0][:, 0:S], ACT.Copy).then_inc(gatherT_ready, 1)
                    for dh in range(2):
                        act.wait_ge(y_psum, 2 * j + dh + 1)
                        act.activation(y_sb[:, dh, :], bank[6 + dh][:, :], ACT.Copy).then_inc(y_ready, 1)

            all_rounds(act, run)

        @block.vector
        def _(dve):
            steps = [0]

            def step(ins):
                steps[0] += 1
                ins.then_inc(vec_step, 1)
                dve.wait_ge(vec_step, steps[0])

            dve.wait_ge(rstd1, 1)
            step(dve.reciprocal(stat[:, 0:2], stat[:, 2:4]))
            for t in range(T):
                dve.tensor_scalar(xn[:, t, :], acc[:, t, :], stat[:, t:t + 1], None, ALU.mult).then_inc(xn_ready, 1)
            dve.wait_ge(params_turned, 1)
            dve.tensor_copy(gains[:, :], bank[4][:, 0:19]).then_inc(gains_ready, 1)
            dve.wait_ge(gains_ready, 1)
            for k in range(KD):
                dve.wait_ge(hT_psum, k // 2 + 1)
                dve.tensor_scalar(hT[:, k, :], bank[k // 2][:, (k % 2) * S:(k % 2) * S + S],
                                  gains[:, G1 + k:G1 + k + 1], None, ALU.mult).then_inc(hT_ready, 1)

            def normalise(g):
                for t in range(T):
                    dve.wait_ge(qk_squared, 2 * g + t + 1)
                    dve.tensor_reduce(stat[:, 64 + 16 * g + 8 * t:72 + 16 * g + 8 * t],
                                      square[:, t * GROUP:(t + 1) * GROUP].rearrange("p (h d) -> p h d", h=AH),
                                      AX, ALU.add).then_inc(qk_summed, 1)
                dve.wait_ge(qk_root, g + 1)
                r = stat[:, 32 + 16 * g:48 + 16 * g]
                step(dve.reciprocal(r, r))
                for t in range(T):
                    v = proj[:, t, g * GROUP:(g + 1) * GROUP].rearrange("p (h d) -> p h d", h=AH)
                    rs = stat[:, 32 + 16 * g + 8 * t:40 + 16 * g + 8 * t].unsqueeze(2)
                    dve.tensor_tensor(v, v, rs.to_broadcast([P, AH, ADH]), ALU.mult).then_inc(qk_normed, 1)

            normalise(0)
            normalise(1)
            dve.wait_ge(rel_in, 32)
            for t in range(T):
                step(dve.memset(rel[t][0:CHUNK, :, 0:CHUNK], MASK_VALUE))

            def add_bias(t):
                if t == 0:
                    for b in range(2):
                        dve.wait_ge(score_psum, b + 1)
                        dve.scalar_tensor_tensor(scores[0][:, b::2, :], bank[b][:, :].rearrange("p (a k) -> p a k", a=4),
                                                 ADH ** -0.5, rel[0][:, b::2, ::-1], ALU.mult, ALU.add)\
                            .then_inc(score_ready, 1)
                else:
                    for n in range(4):
                        b, half = n % 2, n // 2
                        dve.wait_ge(score_psum, 3 + n)
                        dve.scalar_tensor_tensor(scores[1][:, 4 * half + b:4 * half + b + 3:2, :],
                                                 bank[n][:, :].rearrange("p (a k) -> p a k", a=2),
                                                 ADH ** -0.5, rel[1][:, 4 * half + b:4 * half + b + 3:2, ::-1],
                                                 ALU.mult, ALU.add).then_inc(score_ready, 1)
                dve.wait_ge(score_ready, (2, 6)[t])
                m = stat[:, 8 + 8 * t:16 + 8 * t]
                step(dve.tensor_reduce(m, scores[t], AX, ALU.max))
                dve.tensor_scalar(m, m, -1.0, None, ALU.mult).then_inc(max_ready, 1)

            def scale_probs(t):
                dve.wait_ge(exp_ready, t + 1)
                r = stat[:, 96 + 8 * t:104 + 8 * t]
                step(dve.reciprocal(r, r))
                dve.tensor_tensor(scores[t], scores[t], r.unsqueeze(2).to_broadcast([P, AH, P * (t + 1)]), ALU.mult)\
                    .then_inc(prob_ready, 1)

            add_bias(0)
            scale_probs(0)
            dve.wait_ge(abs_z, 3)
            dve.scalar_tensor_tensor(log_a, bank[2][:, :].rearrange("p (t n) -> p t n", t=T), 0.0, decay_tok,
                                     ALU.min, ALU.subtract).then_inc(log_ready, 1)
            add_bias(1)
            scale_probs(1)
            dve.wait_ge(rev_exp, 1)
            dve.tensor_tensor(k_dec, proj[:, :, GQK * GROUP + 256:GQK * GROUP + 512], decay_tok, ALU.mult)\
                .then_inc(kdec_ready, 1)
            dve.wait_ge(gate_sig, 1)
            step(dve.tensor_tensor(out_gate, out_gate, proj[:, :, 5 * GROUP:6 * GROUP], ALU.mult))
            dve.wait_ge(u_psum, 4)
            dve.wait_ge(rev_exp, 2)
            for n in range(NCH):
                t, c = divmod(n, 2)
                ub = bank[(2, 6)[c] + t]
                for pr in range(2):
                    for b in range(2):
                        rows, cols = slice(64 * b, 64 * b + 64), slice(P * b, P * b + P)
                        u = ub[rows, pr * S + P * b:pr * S + P * b + P]
                        if n == 0:
                            ins = dve.tensor_copy(state[rows, n, pr, cols], u)
                        else:
                            ins = dve.scalar_tensor_tensor(state[rows, n, pr, cols], state[rows, n - 1, pr, cols],
                                                           stat[rows, 24 + 4 * pr + n:25 + 4 * pr + n], u,
                                                           ALU.mult, ALU.add)
                ins.then_inc(state_ready, 1)
                dve.wait_ge(state_ready, n + 1)
            for t in range(T):
                dve.wait_ge(gla_squared, t + 1)
                dve.tensor_reduce(stat[:, 112 + 4 * t:116 + 4 * t],
                                  square[:, t * GROUP:(t + 1) * GROUP].rearrange("p (h d) -> p h d", h=GH),
                                  AX, ALU.add).then_inc(gla_summed, 1)
            dve.wait_ge(gla_root, 1)
            step(dve.reciprocal(stat[:, 120:128], stat[:, 120:128]))
            for t in range(T):
                for h in range(GH):
                    cols = slice(h * GDV, (h + 1) * GDV)
                    ins = dve.scalar_tensor_tensor(gla_o[:, t, cols], bank[2 + t][:, cols],
                                                   stat[:, 120 + 4 * t + h:121 + 4 * t + h],
                                                   out_gate[:, t, cols], ALU.mult, ALU.mult)
                ins.then_inc(gla_normed, 1)
            for n in range(4):
                t, dh = divmod(n, 2)
                dve.wait_ge(mix_psum, n + 1)
                v = acc[:, t, dh * GROUP:(dh + 1) * GROUP]
                dve.tensor_tensor(v, bank[(6, 7, 0, 1)[n]][:, :], v, ALU.add).then_inc(x1_ready, 1)
            dve.wait_ge(rstd2, 1)
            step(dve.reciprocal(stat[:, 0:2], stat[:, 2:4]))
            for t in range(T):
                dve.tensor_scalar(xn2[:, t, :], acc[:, t, :], stat[:, t:t + 1], None, ALU.mult).then_inc(xn2_ready, 1)
            dve.wait_ge(xn2_ready, 2)
            for t in range(T):
                step(dve.tensor_copy(h2_parts[0][:, t, :], xn2[:, t, :]))
                step(dve.tensor_tensor(rest, xn2[:, t, :], h2_parts[0][:, t, :], ALU.subtract))
                step(dve.tensor_copy(h2_parts[1][:, t, :], rest))
                step(dve.tensor_tensor(rest, rest, h2_parts[1][:, t, :], ALU.subtract))
                step(dve.tensor_copy(h2_parts[2][:, t, :], rest))
            for t in range(T):
                dve.wait_ge(logit_psum, t + 1)
                logit = rest[:, t * NE:(t + 1) * NE]
                step(dve.tensor_tensor(logit, bank[6 + t][:, 0:NE], b_router[:, :], ALU.add))
                step(dve.max(top_val[:, t, :], logit))
                dve.max_index(top_idx[:, t, :], top_val[:, t, :], logit)
            ins = dve.tensor_scalar(stat[:, 4:6], top_val[:, :, 0], -1.0, None, ALU.mult)
            ins.then_inc(top_ready, 1)
            dve.wait_ge(top_ready, 1)
            step(dve.tensor_copy(top_idx_f[:, :, :], top_idx[:, :, :]))
            for t in range(T):
                ins = dve.tensor_tensor(onehot[:, TOPK * t:TOPK * (t + 1), :],
                                        expert_iota[:, :].unsqueeze(1).to_broadcast([P, TOPK, NE]),
                                        top_idx_f[:, t, 0:TOPK].unsqueeze(2).to_broadcast([P, TOPK, NE]),
                                        ALU.is_equal)
            step(ins)
            for t in range(T):
                ins = dve.tensor_reduce(mask[:, t, :], onehot[:, TOPK * t:TOPK * (t + 1), :].rearrange("p k e -> p e k"),
                                        AX, ALU.add)
            ins.then_inc(mask_ready, 1)
            dve.wait_ge(top_expd, 2)
            step(dve.tensor_reduce(stat[:, 4:6], top_exp[:, :, :], AX, ALU.add))
            step(dve.reciprocal(stat[:, 4:6], stat[:, 4:6]))
            step(dve.tensor_tensor(top_exp[:, :, :], top_exp[:, :, :],
                                   stat[:, 4:6].unsqueeze(2).to_broadcast([P, T, TOPK]), ALU.mult))
            for t in range(T):
                ins = dve.tensor_tensor(gated_hot[:, TOPK * t:TOPK * (t + 1), :], onehot[:, TOPK * t:TOPK * (t + 1), :],
                                        top_exp[:, t, :].unsqueeze(2).to_broadcast([P, TOPK, NE]), ALU.mult)
            step(ins)
            for t in range(T):
                dve.tensor_reduce(gates[:, t, :], gated_hot[:, TOPK * t:TOPK * (t + 1), :].rearrange("p k e -> p e k"),
                                  AX, ALU.add)
            dve.wait_ge(rank_psum, 1)
            rank = rest[:, 0:T * NE].rearrange("p (t e) -> p t e", t=T)
            step(dve.scalar_tensor_tensor(rank, bank[4][:, 0:T * NE].rearrange("p (t e) -> p t e", t=T), 1.0,
                                          mask[:, :, :], ALU.add, ALU.mult))
            for r in range(ROUNDS):
                ins = dve.tensor_scalar(slot_of[:, :, r, :], rank, -1.0 - SLOTS * r, None, ALU.add)
            ins.then_inc(slots_ready, 1)
            dve.tensor_reduce(counts[0:1, 32:40], bank[5][0:1, 0:NE].rearrange("p (q e) -> p q e", e=EPI),
                              AX, ALU.max).then_inc(vec_step, 1)
            steps[0] += 1
            dve.wait_ge(vec_step, steps[0])
            for r in range(1, ROUNDS):
                dve.tensor_scalar(flags[0:1, flag_column(0, r):flag_column(0, r) + ITERS], counts[0:1, 32:40],
                                  float(SLOTS * r), None, ALU.is_gt)
            step(dve.tensor_reduce(counts[0:1, 40:41], counts[0:1, 32:40], AX, ALU.max))
            dve.tensor_scalar(flags[0:1, 24:25], counts[0:1, 40:41], float(SLOTS), None, ALU.is_gt)\
                .then_inc(flags_ready, 1)
            dve.wait_ge(slots_ready, 1)

            def route(j, a, quad, rnd):
                for e in range(2):
                    for t in range(T):
                        n = quad * EPI + 2 * a + e
                        at = slot_of[:, t, rnd, bass.ds(n, 1)]
                        dve.tensor_scalar(pick[a][:, t, e * SLOTS:(e + 1) * SLOTS], slot_iota[:, :], at, None,
                                          ALU.is_equal)
                        dve.tensor_scalar(pick_gated[a][:, t, e * SLOTS:(e + 1) * SLOTS], slot_iota[:, :], at,
                                          gates[:, t, bass.ds(n, 1)], ALU.is_equal, ALU.mult)
                dve.tensor_scalar(bias_pick[a], expert_diff[:, :], pair_first[:, bass.ds(quad * PAIRS + a, 1)], None,
                                  ALU.is_equal).then_inc(route_ready, 1)

            def packed(j, a):
                for n in range(2):
                    dve.wait_ge(pack_psum, 2 * j + n + 1)
                    g = gains[:, G2 + 4 * n:G2 + 4 * n + 4].unsqueeze(2)
                    dve.tensor_tensor(xeT[a][:, 4 * n:4 * n + 4, :], bank[6 + n][:, :].rearrange("p (c s) -> p c s", c=4),
                                      g.to_broadcast([P, 4, P]), ALU.mult).then_inc(pack_ready, 1)

            def hidden(j):
                for hf in range(2):
                    dve.wait_ge(hidden_psum, 4 * j + 2 * hf + 1)
                    dve.tensor_scalar(glu_c[:, hf, :], bank[hf][:, :], LIMIT, None, ALU.min).then_inc(glu_clipped, 1)
                    dve.wait_ge(hidden_psum, 4 * j + 2 * hf + 2)
                    dve.tensor_scalar(lin_c[:, hf, :], bank[2 + hf][:, :], LIMIT, -LIMIT, ALU.min, ALU.max)\
                        .then_inc(lin_clipped, 1)
                for hf in range(2):
                    dve.wait_ge(sig_ready, 2 * j + hf + 1)
                    dve.tensor_tensor(sig[:, hf, :], glu_c[:, hf, :], sig[:, hf, :], ALU.mult).then_inc(glu_ready, 1)
                    dve.wait_ge(glu_ready, 2 * j + hf + 1)
                    dve.scalar_tensor_tensor(act_t[:, hf, :], lin_c[:, hf, :], 1.0, sig[:, hf, :], ALU.add, ALU.mult)\
                        .then_inc(hidden_ready, 1)

            def combine(j):
                for n in range(4):
                    t, dh = divmod(n, 2)
                    dve.wait_ge(comb_psum, 2 * j + t + 1)
                    v = acc[:, t, dh * GROUP:(dh + 1) * GROUP]
                    dve.tensor_tensor(v, bank[4 + n][:, :], v, ALU.add).then_inc(comb_added, 1)

            def run(it, quad, rnd):
                j = it * PAIRS
                first = isinstance(it, int)
                if not first:
                    dve.wait_ge(comb_psum, 2 * j)
                for a in range(PAIRS):
                    route(j + a, a, quad, rnd)
                packed(j, 0)
                hidden(j)
                packed(j + 1, 1)
                combine(j)
                hidden(j + 1)
                combine(j + 1)

            all_rounds(dve, run)
            dve.drain().then_inc(result_ready, 1)

        @block.tensor
        def _(pe):
            pe.wait_ge(ident_ready, 1)
            pe.wait_ge(params_in, 16 * 7)
            pe.transpose(bank[4][:, 0:19], params[0:19, :], ident[0:19, 0:19]).then_inc(params_turned, 1)
            for k in range(KD):
                for t in range(T):
                    pe.wait_ge(xn_ready, t + 1)
                    ins = pe.transpose(bank[k // 2][:, (k % 2) * S + t * P:(k % 2) * S + (t + 1) * P],
                                       xn[:, t, k * P:(k + 1) * P], ident[:, :])
                if k % 2:
                    ins.then_inc(hT_psum, 1)

            def project(g):
                pe.wait_ge(w_in_full[g], 16)
                if g >= 2:
                    pe.wait_ge(proj_ready, 2 * (g - 1))
                if g == 0:
                    pe.wait_ge(gains_ready, 1)
                for t in range(T):
                    for k in range(KD):
                        if g == 0 and t == 0:
                            pe.wait_ge(hT_ready, k + 1)
                        ins = pe.matmul(bank[4 + 2 * (g % 2) + t][:, :], hT[:, k, t * P:(t + 1) * P],
                                        w_buf[g % 2][:, k, :], start=(k == 0), stop=(k == KD - 1))
                    ins.then_inc(proj_psum, 1)

            project(AQ)
            project(AK)
            pe.wait_ge(small_in, 80)
            for k in range(KD):
                ins = pe.matmul(bank[0][0:GRANK, 0:S], w_lr[:, k, :], hT[:, k, :], start=(k == 0), stop=(k == KD - 1))
            ins.then_inc(lr_psum, 1)
            project(AV)
            pe.wait_ge(lr_ready, 1)
            for g in range(2):
                pe.wait_ge(qk_normed, 2 * g + 2)
                for pr in range(4):
                    for t in range(T):
                        ins = pe.transpose(bank[2 * g + pr // 2][:, (pr % 2) * S + t * P:(pr % 2) * S + (t + 1) * P],
                                           proj[:, t, g * GROUP + pr * P:g * GROUP + (pr + 1) * P], ident[:, :])
                    if pr % 2:
                        ins.then_inc(qkT_psum, 1)
            project(GQK)

            def score(t):
                keys = P * (t + 1)
                if t == 0:
                    pe.wait_ge(qkT_ready, 4)
                else:
                    pe.wait_ge(score_ready, 2)
                    pe.wait_ge(log_ready, 1)
                    pe.wait_ge(glaq_ready, 1)
                for half in range(1 if t == 0 else 2):
                    width = 4 if t == 0 else 2
                    for i in range(width):
                        pr = half * width + i
                        for b in range(2):
                            rows = slice(64 * b, 64 * b + 64)
                            ins = pe.matmul(bank[2 * half + b][:, i * keys:(i + 1) * keys],
                                            att_qT[rows, pr, t * P:(t + 1) * P], att_kT[rows, pr, 0:keys],
                                            start=True, stop=True)
                            if i == width - 1:
                                ins.then_inc(score_psum, 1)

            score(0)
            for t in range(T):
                ins = pe.matmul(bank[2][:, t * S:(t + 1) * S], lrT[0:GRANK + 1, t * P:(t + 1) * P], gate_up[:, :],
                                start=True, stop=True)
            ins.then_inc(z_psum, 1)
            pe.wait_ge(proj_ready, 2 * GQK + 2)
            for pr in range(2):
                for t in range(T):
                    c = GQK * GROUP + pr * P
                    ins = pe.transpose(bank[3][:, pr * S + t * P:pr * S + (t + 1) * P], proj[:, t, c:c + P], ident[:, :])
            ins.then_inc(glaq_psum, 1)
            project(GV)
            score(1)
            project(OG)
            pe.wait_ge(proj_ready, 10)
            for t in range(T):
                ins = pe.matmul(bank[4][:, t * S:(t + 1) * S], later[:, :], log_a[:, t, :], start=True, stop=True)
            ins.then_inc(rev_psum, 1)
            for pr in range(2):
                for t in range(T):
                    ins = pe.matmul(bank[5][:, 4 * pr + 2 * t:4 * pr + 2 * t + 2], log_a[:, t, pr * P:(pr + 1) * P],
                                    chunk_of[:, :], start=True, stop=True)
            ins.then_inc(rev_psum, 1)
            pe.wait_ge(prob_ready, 1)
            pe.wait_ge(score_ready, 6)
            for h in range(AH):
                ins = pe.transpose(bank[h // 4][:, (h % 4) * P:(h % 4 + 1) * P], scores[0][:, h, :], ident[:, :])
                if h % 4 == 3:
                    ins.then_inc(probT_psum, 1)
            pe.wait_ge(kdec_ready, 1)
            pe.wait_ge(proj_ready, 12)
            for t in range(T):
                for pr in range(2):
                    for c in range(2):
                        rows = slice(64 * c, 64 * c + 64)
                        col = GV * GROUP + pr * S
                        ins = pe.matmul(bank[(2, 6)[c] + t][:, pr * S:(pr + 1) * S], k_dec[rows, t, pr * P:(pr + 1) * P],
                                        proj[rows, t, col:col + S], start=True, stop=True)
                        if pr:
                            ins.then_inc(u_psum, 1)
            pe.wait_ge(prob_ready, 2)
            pe.wait_ge(probT_ready, 2)
            pe.wait_ge(rev_exp, 2)
            for kt in range(2):
                for h in range(AH):
                    ins = pe.transpose(bank[4 * kt + h // 4][:, (h % 4) * P:(h % 4 + 1) * P],
                                       scores[1][:, h, kt * P:(kt + 1) * P], ident[:, :])
                    if h % 4 == 3:
                        ins.then_inc(probT_psum, 1)
            for n in range(NCH):
                t, c = divmod(n, 2)
                pe.wait_ge(state_ready, 4 if n == 0 else n + 1)
                for pr in range(2):
                    ins = pe.matmul(bank[2 + t][64 * c:64 * c + 64, pr * S:(pr + 1) * S],
                                    gla_qT[:, pr, n * CHUNK:(n + 1) * CHUNK], state[:, n, pr, :], start=True, stop=True)
                if c:
                    ins.then_inc(gla_psum, 1)
            pe.wait_ge(probT_ready, 6)
            for pr in range(4):
                for b in range(2):
                    h = 2 * pr + b
                    o_ = bank[pr // 2][64 * b:64 * b + 64, (pr % 2) * S:(pr % 2) * S + S]
                    vc = AV * GROUP + h * ADH
                    pe.matmul(o_, proj[:, 0, vc:vc + ADH], probT[0][:, h, :], start=True, stop=False)
                    ins = pe.matmul(o_[:, P:S], proj[:, 1, vc:vc + ADH], probT[1][:, h, :], start=False, stop=True)
                if pr % 2:
                    ins.then_inc(att_psum, 1)
            pe.wait_ge(gla_normed, 2)
            for h in range(GH):
                for t in range(T):
                    ins = pe.transpose(bank[4 + h // 2][:, (h % 2) * S + t * P:(h % 2) * S + (t + 1) * P],
                                       gla_o[:, t, h * GDV:(h + 1) * GDV], ident[:, :])
                if h % 2:
                    ins.then_inc(glaT_psum, 1)
            pe.wait_ge(att_ready, 2)
            pe.wait_ge(glaT_ready, 2)
            for b in range(2):
                pe.wait_ge(w_out_full[b], 16)
            for n in range(4):
                t, dh = divmod(n, 2)
                for k in range(KD):
                    ins = pe.matmul(bank[(6, 7, 0, 1)[n]][:, :], mixT[:, k, t * P:(t + 1) * P],
                                    w_out_sb[:, k, dh * GROUP:(dh + 1) * GROUP], start=(k == 0), stop=(k == KD - 1))
                ins.then_inc(mix_psum, 1)
            for k in range(KD):
                for t in range(T):
                    pe.wait_ge(xn2_ready, t + 1)
                    ins = pe.transpose(bank[2 + k // 2][:, (k % 2) * S + t * P:(k % 2) * S + (t + 1) * P],
                                       xn2[:, t, k * P:(k + 1) * P], ident[:, :])
                if k % 2:
                    ins.then_inc(h2T_psum, 1)
            pe.wait_ge(h2T_ready, KD)
            for t in range(T):
                for k in range(KD):
                    ins = pe.matmul(bank[6 + t][:, 0:NE], h2T[:, k, t * P:(t + 1) * P], w_router[:, k, :],
                                    start=(k == 0), stop=(k == KD - 1))
                ins.then_inc(logit_psum, 1)
            pe.wait_ge(mask_ready, 1)
            pe.matmul(bank[5][0:1, 0:NE], ones[:, 0:1], mask[:, 0, :], start=True, stop=False)
            pe.matmul(bank[5][0:1, 0:NE], ones[:, 0:1], mask[:, 1, :], start=False, stop=True)
            pe.matmul(bank[4][:, 0:NE], before[:, :], mask[:, 0, :], start=True, stop=True)
            pe.matmul(bank[4][:, NE:2 * NE], ones[:, :], mask[:, 0, :], start=True, stop=False)
            pe.matmul(bank[4][:, NE:2 * NE], before[:, :], mask[:, 1, :], start=False, stop=True).then_inc(rank_psum, 1)
            pe.wait_ge(flags_ready, 1)

            def pack(j, a, first):
                pe.wait_ge(route_ready, j + 1)
                if not first and a == 0:
                    pe.wait_ge(comb_added, 4 * j)
                for c in range(KD):
                    for t in range(T):
                        for i in range(3):
                            ins = pe.matmul(bank[6 + c // 4][:, (c % 4) * P:(c % 4 + 1) * P],
                                            h2_parts[i][:, t, c * P:(c + 1) * P], pick[a][:, t, :],
                                            start=(t == 0 and i == 0), stop=(t == T - 1 and i == 2))
                            if a == 1 and c == 0 and t == 0 and i == 0:
                                ins.then_inc(chunks_used, 1)
                    if c % 4 == 3:
                        ins.then_inc(pack_psum, 1)

            def arrived(it, c):
                per = ITER_CHUNKS // RING
                pe.wait_ge(ring_full[c % RING], it * (16 * per) + 16 * (c // RING + 1))

            def up(it, j, a, first):
                pe.wait_ge(pack_ready, 2 * j + 2)
                if not first:
                    pe.wait_ge(hidden_ready, 2 * j)
                    pe.wait_ge(gatherT_ready, j)
                for n in range(4):
                    pe.matmul(bank[n][:, :], bias_pick[a], bias_parts[:, n * GROUP:(n + 1) * GROUP],
                              start=True, stop=False, skip_group_check=True)
                for k in range(KD):
                    c = a * JOB_CHUNKS + 2 * k
                    arrived(it, c)
                    arrived(it, c + 1)
                    for n in (0, 2, 1, 3):
                        for e in range(2):
                            ins = pe.matmul(bank[n][64 * e:64 * e + 64, :], xeT[a][:, k, 64 * e:64 * e + 64],
                                            ring[:, (c + e) % RING, n * GROUP:(n + 1) * GROUP],
                                            start=False, stop=(k == KD - 1), skip_group_check=True)
                            if n == 3 and (e == 0 or k < KD - 1):
                                ins.then_inc(chunks_used, 1)
                        if k == KD - 1:
                            ins.then_inc(hidden_psum, 1)

            def turn(j, a, first):
                if not first:
                    pe.wait_ge(comb_added, 4 * j)
                for hf in range(2):
                    pe.wait_ge(hidden_ready, 2 * j + hf + 1)
                    for i in range(4):
                        ins = pe.transpose(bank[4 + hf][:, i * P:(i + 1) * P], act_t[:, hf, i * P:(i + 1) * P], ident[:, :])
                        if a == 1 and hf == 0 and i == 0:
                            ins.then_inc(chunks_used, 1)
                    ins.then_inc(hiddenT_psum, 1)
                for t in range(T):
                    ins = pe.transpose(bank[0][:, t * P:(t + 1) * P], pick_gated[a][:, t, :], ident[:, :])
                ins.then_inc(gatherT_psum, 1)

            def down(it, j, a, first):
                pe.wait_ge(pack_ready, 2 * j + 4 if a == 0 else 2 * j + 2)
                pe.wait_ge(hiddenT_ready, 2 * j + 2)
                for dh in range(2):
                    c0 = 2 * D + dh * GROUP
                    pe.matmul(bank[6 + dh][:, :], bias_pick[a], bias_parts[:, c0:c0 + GROUP],
                              start=True, stop=False, skip_group_check=True)
                for i in range(KD // 2):
                    c = a * JOB_CHUNKS + 2 * KD + 2 * i
                    arrived(it, c)
                    arrived(it, c + 1)
                    for kk in range(2):
                        last = i == KD // 2 - 1 and kk == 1
                        for dh in range(2):
                            for e in range(2):
                                f = kk * D + dh * GROUP
                                ins = pe.matmul(bank[6 + dh][64 * e:64 * e + 64, :],
                                                actT[:, 2 * i + kk, 64 * e:64 * e + 64],
                                                ring[:, (c + e) % RING, f:f + GROUP], start=False, stop=last,
                                                skip_group_check=True)
                                if kk == 1 and dh == 1 and (e == 0 or not last):
                                    ins.then_inc(chunks_used, 1)
                            if last:
                                ins.then_inc(y_psum, 1)

            def spread(j):
                pe.wait_ge(gatherT_ready, j + 1)
                for n in range(4):
                    t, dh = divmod(n, 2)
                    pe.wait_ge(y_ready, 2 * j + 2)
                    ins = pe.matmul(bank[4 + n][:, :], gatherT[:, t * P:(t + 1) * P], y_sb[:, dh, :],
                                    start=True, stop=True)
                    if n == 0:
                        ins.then_inc(chunks_used, 1)
                    if dh == 1:
                        ins.then_inc(comb_psum, 1)

            def run(it, quad, rnd):
                first = isinstance(it, int)
                j = it * PAIRS
                pack(j, 0, first)
                up(it, j, 0, first)
                pack(j + 1, 1, first)
                turn(j, 0, first)
                down(it, j, 0, first)
                spread(j)
                up(it, j + 1, 1, False)
                turn(j + 1, 1, False)
                down(it, j + 1, 1, False)
                spread(j + 1)

            all_rounds(pe, run)


_INS = ['x', 'norm1_g', 'w_in', 'gla_gate_up', 'gla_gate_bias', 'gla_norm_g', 'q_norm_g', 'k_norm_g',
        'rel_bias', 'w_out', 'norm2_g', 'router_w', 'router_b', 'moe_w_in', 'moe_b_in', 'moe_w_out', 'moe_b_out']
_OUTS = [((1, S, D), 'float32')]


def kernel(**inputs):
    import numpy as _np
    import concourse.bacc as _bacc
    from concourse import mybir as _mybir
    from concourse.bass_utils import run_bass_kernel_spmd as _run

    nc = _bacc.Bacc("TRN2", target_bir_lowering=False, num_devices=1)
    arrays, args = {}, []
    for name in _INS:
        a = _np.ascontiguousarray(inputs[name])
        arrays[f"in_{name}_dram"] = a
        args.append(nc.dram_tensor(f"in_{name}_dram", a.shape, _mybir.dt.from_np(a.dtype), kind="ExternalInput").ap())
    for i, (shape, dtype) in enumerate(_OUTS):
        dt = _mybir.dt.from_np(_np.dtype(dtype))
        args.append(nc.dram_tensor(f"out_{i}_dram", shape, dt, kind="ExternalOutput").ap())
    build(nc, *args)
    r = _run(nc, [arrays], core_ids=[0])
    return r.results[0]["out_0_dram"]
```

```python
from contextlib import ExitStack

import concourse.bass as bass
from concourse import mybir

P = 128
D = 1024
S = 256
T = S // P
CHUNK = 64
NCH = S // CHUNK
KD = D // P
EPS = 1e-6
GH, GDK, GDV, GRANK, GTAU = 4, 64, 128, 16, 16.0
AH, ADH = 8, 64
REL_CLIP = 256
MASK_VALUE = -1e30
NE, TOPK, F = 32, 4, 1024
ALPHA, LIMIT = 1.702, 7.0
GROUP = 512
AQ, AK, AV, GQK, GV, OG = range(6)
GROUP_COL = (1552, 2064, 2576, 0, 512, 1040)
LR_COL = 1024

SLOTS = 64
ROUNDS = S // SLOTS
PAIRS = 2
EPI = 2 * PAIRS
ITERS = NE // EPI
CHUNK_F = 2048
RING = 16
JOB_CHUNKS = 2 * KD + KD
ITER_CHUNKS = PAIRS * JOB_CHUNKS
EXTRA = 4
FIRST_EXTRA = RING - EXTRA

F32 = mybir.dt.float32
BF16 = mybir.dt.bfloat16
I32 = mybir.dt.int32
U32 = mybir.dt.uint32
ALU = mybir.AluOpType
ACT = mybir.ActivationFunctionType
AX = mybir.AxisListType.X


def build(nc, x, norm1_g, w_in, gla_gate_up, gla_gate_bias, gla_norm_g, q_norm_g, k_norm_g,
          rel_bias, w_out, norm2_g, router_w, router_b, moe_w_in, moe_b_in, moe_w_out,
          moe_b_out, out):
    with ExitStack() as ctx:
        def sb(name, shape, dt=F32):
            return ctx.enter_context(nc.sbuf_tensor(name, shape, dt))

        def sem(name):
            return ctx.enter_context(nc.semaphore(name))

        ring = sb("ring", [P, RING, CHUNK_F])
        acc = sb("acc", [P, T, D])
        area = sb("area", [P, 15104])
        bias_parts = sb("bias_parts", [P, 3 * D], BF16)
        ident = sb("ident", [P, P])
        later = sb("later", [P, P])
        before = sb("before", [P, P])
        ones = sb("ones", [P, P])
        chunk_of = sb("chunk_of", [P, 2])
        eps = sb("eps", [P, 1])
        slot_iota = sb("slot_iota", [P, SLOTS])
        expert_iota = sb("expert_iota", [P, NE])
        expert_diff = sb("expert_diff", [P, P])
        pair_first = sb("pair_first", [P, NE // 2])
        gains = sb("gains", [P, 19])
        w_router = sb("w_router", [P, KD, NE])
        b_router = sb("b_router", [P, NE])
        stat = sb("stat", [P, 128])
        gates = sb("gates", [P, T, NE])
        mask = sb("mask", [P, T, NE])
        slot_of = sb("slot_of", [P, T, ROUNDS, NE])
        top_val = sb("top_val", [P, T, 8])
        top_idx = sb("top_idx", [P, T, 8], U32)
        top_idx_f = sb("top_idx_f", [P, T, 8])
        top_exp = sb("top_exp", [P, T, TOPK])
        counts = sb("counts", [1, 64])
        flags = sb("flags", [1, 32], I32)

        def part(base, off, *dims):
            n = 1
            for d in dims:
                n *= d
            v = base[:, off:off + n]
            if len(dims) == 1:
                return v
            names = "abc"[:len(dims)]
            return v.rearrange("p (%s) -> p %s" % (" ".join(names), " ".join(names)),
                               **{c: d for c, d in zip(names, dims)})

        hT = part(area, 0, KD, S)
        mixT = hT
        proj = part(area, 2048, T, 6 * GROUP)
        o = 8192
        gla_qT = part(area, o, 2, S)
        log_a = part(area, o + 512, T, S)
        decay_tok = part(area, o + 1024, T, S)
        k_dec = part(area, o + 1536, T, S)
        state = part(area, o + 2048, NCH, 2, S)
        x_squares = part(area, 2048, T, D)
        gla_o = part(area, o + 4096, T, GROUP)
        out_gate = part(area, o + 5120, T, GROUP)
        lrT = part(area, o + 6144, S)
        low_rank = part(area, o + 4096, T, GRANK)
        w_lr = part(area, o + 6400, KD, GRANK)
        gate_up = area[0:GRANK + 1, o + 6528:o + 6784]
        params = part(area, o + 6784, P)
        spare = ring[:, :, :].rearrange("p s f -> p (s f)")
        A0 = 6 * CHUNK_F
        scores = [part(spare, A0, AH, P), part(spare, A0 + 1024, AH, S)]
        probT = [part(spare, A0 + 3072, AH, S), part(spare, A0 + 5120, AH, P)]
        rel = [part(spare, A0 + 6144, AH, P), part(spare, A0 + 7168, AH, S)]
        att_qT = part(spare, A0 + 9216, AH // 2, S)
        att_kT = part(spare, A0 + 10240, AH // 2, S)
        square = part(spare, A0 + 11264, 2 * GROUP)
        bias_raw = part(spare, A0, 3 * D)
        bias_rest = part(spare, A0 + 3 * D, 3 * D)
        GROUP_SLOT = (12, 14, 0, 2, 4, 0)
        w_buf = [part(spare, slot * CHUNK_F, KD, GROUP) for slot in GROUP_SLOT]
        w_out_sb = part(spare, 12 * CHUNK_F, KD, D)
        extra = [part(area, at, CHUNK_F) for at in (2048, 0, 11264, 9216)]
        glu_c = part(area, 0, 2, GROUP)
        sig = part(area, 1024, 2, GROUP)
        lin_c = part(area, 2048, 2, GROUP)
        act_t = part(area, 3072, 2, GROUP)
        h2_parts = [part(area, 4096 + 1024 * i, 1024).bitcast(BF16).rearrange("p (t d) -> p t d", t=T)
                    for i in range(3)]
        x1T = part(area, 7168, KD, S)
        xeT = [part(area, 7168 + 1024 * i, KD, P) for i in range(PAIRS)]
        h2_rest = part(area, 9216, D)
        squares2 = part(area, 10240, 512).bitcast(BF16)
        actT = part(area, 9216, KD, P)
        y_sb = part(area, 10240, 2, GROUP)
        gatherT = part(area, 13376, S)
        pick = [part(area, 13632 + 128 * i, 128).bitcast(BF16).rearrange("p (t s) -> p t s", t=T)
                for i in range(PAIRS)]
        pick_gated = [part(area, 13888 + 256 * i, T, P) for i in range(PAIRS)]
        bias_pick = [part(area, 14400 + 64 * i, 64).bitcast(BF16) for i in range(PAIRS)]
        onehot = part(area, 14528, T * TOPK, NE)
        gated_hot = part(area, 14784, T * TOPK, NE)
        route_tmp = part(area, 15040, T, NE)

        bank = [ctx.enter_context(nc.psum_tensor(f"bank{i}", [P, 512], F32)) for i in range(8)]

        g1_in, g1_turned, g1_ready = map(sem, ("g1_in", "g1_turned", "g1_ready"))
        x_in0, params_in, small_in, rel_in, bias_in = map(sem, ("x_in0", "params_in", "small_in", "rel_in", "bias_in"))
        x_in = [x_in0, sem("x_in1")]
        out_stored = sem("out_stored")
        w_first_full = [sem(f"w_first_full{i}") for i in range(4)]
        w_in_full = [None] + [sem(f"w_in_full{g}") for g in range(1, 6)]
        w_out_full = [sem(f"w_out_full{b}") for b in range(2)]
        extra_full = [sem(f"extra_full{i}") for i in range(EXTRA)]
        ring_full = [sem(f"ring_full{s}") for s in range(RING)]
        result_ready = sem("result_ready")
        pool_step, ident_ready, consts_ready, bias_split = map(sem, ("pool_step", "ident_ready", "consts_ready", "bias_split"))
        vec_step, act_step = sem("vec_step"), sem("act_step")
        sq1, root1, rstd1 = map(sem, ("sq1", "root1", "rstd1"))
        router_scaled, low_rank_ready = map(sem, ("router_scaled", "low_rank_ready"))
        params_turned, gains_ready = map(sem, ("params_turned", "gains_ready"))
        hT_psum, hT_ready = map(sem, ("hT_psum", "hT_ready"))
        proj_psum, proj_ready = map(sem, ("proj_psum", "proj_ready"))
        lr_psum, lrT_psum, lr_ready, z_psum, abs_z, log_ready = map(sem, ("lr_psum", "lrT_psum", "lr_ready", "z_psum", "abs_z", "log_ready"))
        qk_squared, qk_summed, qk_root, qk_normed = map(sem, ("qk_squared", "qk_summed", "qk_root", "qk_normed"))
        qkT_psum, qkT_ready = map(sem, ("qkT_psum", "qkT_ready"))
        score_psum, score_ready, max_ready, exp_ready, prob_ready = map(
            sem, ("score_psum", "score_ready", "max_ready", "exp_ready", "prob_ready"))
        glaq_psum, glaq_ready = map(sem, ("glaq_psum", "glaq_ready"))
        rev_psum, rev_exp, kdec_ready = map(sem, ("rev_psum", "rev_exp", "kdec_ready"))
        probT_psum, probT_ready = map(sem, ("probT_psum", "probT_ready"))
        u_psum, state_ready = map(sem, ("u_psum", "state_ready"))
        att_psum, att_ready = map(sem, ("att_psum", "att_ready"))
        gate_sig, gla_psum, gla_squared, gla_summed, gla_root, gla_normed = map(
            sem, ("gate_sig", "gla_psum", "gla_squared", "gla_summed", "gla_root", "gla_normed"))
        glaT_psum, glaT_ready = map(sem, ("glaT_psum", "glaT_ready"))
        mix_psum, x1_ready = map(sem, ("mix_psum", "x1_ready"))
        sq2, root2, rstd2 = map(sem, ("sq2", "root2", "rstd2"))
        part0_ready, rest_ready, part1_ready, h2_ready = map(
            sem, ("part0_ready", "rest_ready", "part1_ready", "h2_ready"))
        x1T_psum, x1T_act, x1T_dve, logit_psum, top_ready, top_expd = map(
            sem, ("x1T_psum", "x1T_act", "x1T_dve", "logit_psum", "top_ready", "top_expd"))
        mask_ready, rank_psum, slots_ready, flags_ready = map(
            sem, ("mask_ready", "rank_psum", "slots_ready", "flags_ready"))
        gated_ready, bias_pick_ready = map(sem, ("gated_ready", "bias_pick_ready"))
        chunks_used, route_ready, pack_psum, pack_ready, hidden_psum = map(
            sem, ("chunks_used", "route_ready", "pack_psum", "pack_ready", "hidden_psum"))
        glu_clipped, lin_clipped, sig_ready, glu_ready, hidden_ready = map(
            sem, ("glu_clipped", "lin_clipped", "sig_ready", "glu_ready", "hidden_ready"))
        hiddenT_psum, hiddenT_ready, gatherT_psum, gatherT_ready = map(
            sem, ("hiddenT_psum", "hiddenT_ready", "gatherT_psum", "gatherT_ready"))
        y_psum, y_ready, comb_psum, comb_added = map(sem, ("y_psum", "y_ready", "comb_psum", "comb_added"))

        G1, G2, GN, GQ, GK = 0, KD, 2 * KD, 2 * KD + 1, 2 * KD + 2
        block = ctx.enter_context(nc.Block())

        def flag_column(quad, rnd):
            return (rnd - 1) * ITERS + quad

        def all_rounds(eng, run, no_more=None):
            run(0, 0, 0)
            with eng.Fori(1, ITERS) as it:
                run(it, it, 0)
            eng.wait_ge(flags_ready, 1)
            with eng.If(eng.value_load(flags[0:1, 24:25], min_val=0, max_val=1) != 0):
                done = eng.alloc_register("iterations_done")
                eng.reg_mov(done, ITERS)
                for rnd in range(1, ROUNDS):
                    with eng.Fori(0, ITERS) as quad:
                        col = eng.snap(quad + (rnd - 1) * ITERS)
                        flag = eng.value_load(flags[0:1, bass.ds(col, 1)], min_val=0, max_val=1)
                        with eng.If(flag != 0):
                            it = eng.snap(done, min_val=ITERS, max_val=ITERS * ROUNDS)
                            run(it, quad, rnd)
                            eng.reg_add(done, done, 1)
                        with eng.Else():
                            eng.nop()
                        eng.nop()
            with eng.Else():
                if no_more:
                    no_more()
                eng.nop()
            eng.nop()

        @block.sync
        def _(sp):
            for t in range(T):
                sp.dma_start(acc[:, t, :], x[0, t * P:(t + 1) * P, :]).then_inc(x_in[t], 16)

            def load_group(g):
                c = GROUP_COL[g]
                sp.dma_start(w_buf[g], w_in[0, :, c:c + GROUP].rearrange("(k p) n -> p k n", p=P))\
                    .then_inc(w_in_full[g], 16)

            def fill(buf, full, quad, c):
                job, r = divmod(c, JOB_CHUNKS)
                if r < 2 * KD:
                    k, e = divmod(r, 2)
                    src = moe_w_in[0, bass.ds(quad * EPI + 2 * job + e, 1), k * P:(k + 1) * P, :]
                    dst = buf.rearrange("p (a f) -> p a f", a=1)
                    src = src.rearrange("a p f -> p a f")
                else:
                    k, e = divmod(r - 2 * KD, 2)
                    src = moe_w_out[0, bass.ds(quad * EPI + 2 * job + e, 1), 2 * k * P:2 * (k + 1) * P, :]
                    src = src.rearrange("a (k p) d -> p (a k) d", p=P)
                    dst = buf.rearrange("p (k d) -> p k d", k=2)
                sp.dma_start(dst, src).then_inc(full, 16)

            def fill_ring(slot, quad, c):
                fill(ring[:, slot, :], ring_full[slot], quad, c)

            def fill_extra(i):
                fill(extra[i], extra_full[i], 0, FIRST_EXTRA + i)

            for i in range(4):
                c = GROUP_COL[0]
                sp.dma_start(w_buf[0][:, 2 * i:2 * i + 2, :],
                             w_in[0, 2 * i * P:2 * (i + 1) * P, c:c + GROUP].rearrange("(k p) n -> p k n", p=P))\
                    .then_inc(w_first_full[i], 16)
            for g in range(1, 5):
                load_group(g)
            for b in range(2):
                sp.wait_ge(proj_psum, 2 * (b + 1))
                sp.dma_start(w_out_sb[:, 4 * b:4 * b + 4, :],
                             w_out[0, b * 512:(b + 1) * 512, :].rearrange("(k p) n -> p k n", p=P))\
                    .then_inc(w_out_full[b], 16)
            sp.wait_ge(proj_psum, 2 * (AV + 1))
            load_group(OG)
            for g, slots in ((GQK, (2, 3)), (GV, (4, 5)), (OG, (0, 1))):
                sp.wait_ge(proj_psum, 2 * (g + 1))
                for slot in slots:
                    fill_ring(slot, 0, slot)
            sp.wait_ge(gla_summed, 2)
            sp.wait_ge(att_psum, 2)
            for slot in range(6, 12):
                fill_ring(slot, 0, slot)
            fill_extra(0)
            sp.wait_ge(glaT_psum, 2)
            fill_extra(2)
            sp.wait_ge(mix_psum, 4)
            fill_extra(1)
            for slot in range(12, RING):
                fill_ring(slot, 0, slot + RING)
            sp.wait_ge(h2_ready, 2)
            fill_extra(3)

            def run(it, quad, rnd):
                first = isinstance(it, int)
                for c in range(RING if first else 0, ITER_CHUNKS):
                    if first and FIRST_EXTRA + RING <= c < 2 * RING:
                        continue
                    sp.wait_ge(chunks_used, it * ITER_CHUNKS + c - RING + 1)
                    fill_ring(c % RING, quad, c)

            def store(n):
                dh, t = divmod(n, 2)
                cols = slice(dh * GROUP, (dh + 1) * GROUP)
                sp.dma_start(out[0, t * P:(t + 1) * P, cols], acc[:, t, cols]).then_inc(out_stored, 16)

            def store_after_round_0():
                for n in range(4):
                    sp.wait_ge(comb_added, 4 * PAIRS * ITERS - 3 + n)
                    store(n)

            all_rounds(sp, run, store_after_round_0)
            sp.wait_ge(result_ready, 1)
            with sp.If(sp.value_load(flags[0:1, 24:25], min_val=0, max_val=1) != 0):
                for n in range(4):
                    store(n)
            with sp.Else():
                sp.nop()
            sp.wait_ge(out_stored, 16 * 4)

        @block.gpsimd
        def _(pool):
            steps = [0]

            def step(ins):
                steps[0] += 1
                ins.then_inc(pool_step, 1)
                pool.wait_ge(pool_step, steps[0])

            step(pool.memset(ident[:, :], 0.0))
            step(pool.memset(eps[:, :], EPS))
            pool.affine_select(out=ident[:, :], in_=ident[:, :], compare_op=ALU.not_equal, fill=1.0,
                               base=0, pattern=[[-1, P]], channel_multiplier=1).then_inc(ident_ready, 1)
            pool.wait_ge(ident_ready, 1)
            step(pool.memset(ones[:, :], 1.0))
            step(pool.memset(lrT[0:32, :], 1.0))
            step(pool.memset(chunk_of[:, :], 0.0))
            step(pool.memset(state[:, :, :, :], 0.0))
            step(pool.memset(chunk_of[0:64, 0:1], 1.0))
            step(pool.memset(chunk_of[64:128, 1:2], 1.0))
            step(pool.affine_select(out=later[:, :], in_=ones[:, :], compare_op=ALU.is_gt, fill=0.0,
                                    base=0, pattern=[[-1, P]], channel_multiplier=1))
            step(pool.affine_select(out=before[:, :], in_=ones[:, :], compare_op=ALU.is_gt, fill=0.0,
                                    base=0, pattern=[[1, P]], channel_multiplier=-1))
            step(pool.memset(later[64:128, 0:64], 0.0))
            step(pool.iota(slot_iota[:, :], [[1, SLOTS]], base=0, channel_multiplier=0,
                           allow_small_or_imprecise_dtypes=True))
            step(pool.iota(expert_iota[:, :], [[1, NE]], base=0, channel_multiplier=0,
                           allow_small_or_imprecise_dtypes=True))
            step(pool.iota(pair_first[:, :], [[2, NE // 2]], base=0, channel_multiplier=0,
                           allow_small_or_imprecise_dtypes=True))
            for i in range(3):
                step(pool.iota(expert_diff[32 * i:32 * i + 32, :], [[-1, 2], [0, 64]], base=0,
                               channel_multiplier=1, allow_small_or_imprecise_dtypes=True))
            step(pool.memset(expert_diff[96:128, :], -5.0))
            pool.memset(bias_parts[96:128, :], 0.0).then_inc(consts_ready, 1)

        @block.scalar
        def _(act):
            act.dma_start(params[0:8, :], norm1_g[0].rearrange("(k p) -> k p", p=P)).then_inc(g1_in, 16)
            act.dma_start(params[8:16, :], norm2_g[0].rearrange("(k p) -> k p", p=P)).then_inc(params_in, 16)
            act.dma_start(params[16:17, :], gla_norm_g).then_inc(params_in, 16)
            for row, g in ((17, q_norm_g), (18, k_norm_g)):
                for b in range(2):
                    act.dma_start(params[row:row + 1, b * 64:b * 64 + 64], g).then_inc(params_in, 16)
            act.dma_start(w_lr[:, :, :], w_in[0, :, LR_COL:LR_COL + GRANK].rearrange("(k p) n -> p k n", p=P))\
                .then_inc(small_in, 16)
            act.dma_start(area[0:GRANK, o + 6528:o + 6784], gla_gate_up[0]).then_inc(small_in, 16)
            act.dma_start(area[GRANK:GRANK + 1, o + 6528:o + 6784], gla_gate_bias).then_inc(small_in, 16)
            act.dma_start(w_router[:, :, :], router_w[0].rearrange("(k p) n -> p k n", p=P)).then_inc(small_in, 16)
            act.dma_start(b_router[:, :], bass.AP(router_b.tensor, router_b.offset, [[0, P], [1, NE]]))\
                .then_inc(small_in, 16)
            for t in range(T):
                keys = P * (t + 1)
                off = REL_CLIP + P * t - (keys - 1)
                act.dma_start(rel[t], bass.AP(rel_bias.tensor, rel_bias.offset + off,
                                              [[1, P], [2 * REL_CLIP + 1, AH], [1, keys]])).then_inc(rel_in, 16)
            for i in range(3):
                act.dma_start(bias_raw[32 * i:32 * i + 32, 0:2 * D], moe_b_in[0]).then_inc(bias_in, 16)
                act.dma_start(bias_raw[32 * i:32 * i + 32, 2 * D:3 * D], moe_b_out[0]).then_inc(bias_in, 16)

            act.wait_ge(ident_ready, 1)
            for t in range(T):
                act.wait_ge(x_in[t], 16)
                act.activation(x_squares[:, t, :], acc[:, t, :], ACT.Square, accum_out=stat[:, t:t + 1])\
                    .then_inc(sq1, 1)
            act.wait_ge(sq1, 2)
            act.activation(stat[:, 2:4], stat[:, 0:2], ACT.Sqrt, bias=eps[:, 0:1], scale=1.0 / D).then_inc(root1, 1)
            act.wait_ge(rstd1, 1)

            def project_out(g, tiles=(0, 1)):
                for t in tiles:
                    act.wait_ge(proj_psum, 2 * g + t + 1)
                    act.activation(proj[:, t, g * GROUP:(g + 1) * GROUP], bank[4 + 2 * (g % 2) + t][:, :],
                                   ACT.Copy, scale=stat[:, t:t + 1]).then_inc(proj_ready, 1)

            def squares(g):
                act.wait_ge(proj_ready, 2 * g + 2)
                if g:
                    act.wait_ge(qk_summed, 2 * g)
                for t in range(T):
                    act.activation(square[:, t * GROUP:(t + 1) * GROUP], proj[:, t, g * GROUP:(g + 1) * GROUP],
                                   ACT.Square).then_inc(qk_squared, 1)
                act.wait_ge(qk_summed, 2 * g + 2)
                act.activation(stat[:, 32 + 16 * g:48 + 16 * g], stat[:, 64 + 16 * g:80 + 16 * g], ACT.Sqrt,
                               bias=eps[:, 0:1], scale=1.0 / ADH).then_inc(qk_root, 1)

            project_out(AQ)
            squares(0)
            project_out(AK)
            squares(1)
            act.wait_ge(lr_psum, 1)
            for t in range(T):
                act.activation(low_rank[:, t, :], bank[0][:, t * GRANK:(t + 1) * GRANK], ACT.Copy,
                               scale=stat[:, t:t + 1]).then_inc(low_rank_ready, 1)
            act.wait_ge(lrT_psum, 1)
            act.wait_ge(consts_ready, 1)
            act.activation(lrT[0:GRANK, :], bank[1][0:GRANK, 0:S], ACT.Copy).then_inc(lr_ready, 1)
            project_out(AV)
            for n in range(4):
                act.wait_ge(qkT_psum, n + 1)
                dst = (att_qT, att_kT)[n // 2]
                gain = (GQ, GK)[n // 2]
                act.activation(dst[:, 2 * (n % 2):2 * (n % 2) + 2, :],
                               bank[n][:, :].rearrange("p (a b) -> p a b", a=2), ACT.Copy,
                               scale=gains[:, gain:gain + 1]).then_inc(qkT_ready, 1)
            project_out(GQK)
            act.wait_ge(glaq_psum, 1)
            act.activation(gla_qT, bank[3][:, :].rearrange("p (a b) -> p a b", a=2), ACT.Copy,
                           scale=GDK ** -0.5).then_inc(glaq_ready, 1)

            def exps(t):
                act.wait_ge(max_ready, t + 1)
                for h in range(AH):
                    ins = act.activation(scores[t][:, h, :], scores[t][:, h, :], ACT.Exp,
                                         bias=stat[:, 8 + 8 * t + h:9 + 8 * t + h],
                                         accum_out=stat[:, 96 + 8 * t + h:97 + 8 * t + h])
                ins.then_inc(exp_ready, 1)

            exps(0)
            act.wait_ge(z_psum, 1)
            z = bank[2][:, :].rearrange("p (t n) -> p t n", t=T)
            act.activation(decay_tok, z, ACT.Abs).then_inc(abs_z, 1)
            act.wait_ge(abs_z, 1)
            act.activation(k_dec, decay_tok, ACT.Exp, scale=-1.0).then_inc(abs_z, 1)
            act.wait_ge(abs_z, 2)
            act.wait_ge(consts_ready, 1)
            act.activation(decay_tok, k_dec, ACT.Ln, bias=ones[:, 0:1]).then_inc(abs_z, 1)
            project_out(GV)
            exps(1)
            project_out(OG, (0,))
            act.wait_ge(rev_psum, 2)
            act.activation(decay_tok, bank[4][:, :].rearrange("p (t n) -> p t n", t=T), ACT.Exp,
                           scale=1.0 / GTAU).then_inc(rev_exp, 1)
            act.activation(stat[:, 24:32], bank[5][:, 0:8], ACT.Exp, scale=1.0 / GTAU).then_inc(rev_exp, 1)
            for n in range(2):
                act.wait_ge(probT_psum, n + 1)
                act.activation(probT[0][:, 4 * n:4 * n + 4, 0:P],
                               bank[n][:, :].rearrange("p (a b) -> p a b", a=4), ACT.Copy).then_inc(probT_ready, 1)
            project_out(OG, (1,))
            act.wait_ge(proj_ready, 12)
            act.activation(out_gate, proj[:, :, 5 * GROUP:6 * GROUP], ACT.Sigmoid).then_inc(gate_sig, 1)
            for n in range(4):
                act.wait_ge(probT_psum, n + 3)
                dst = probT[0][:, 4 * n:4 * n + 4, P:S] if n < 2 else probT[1][:, 4 * (n - 2):4 * (n - 2) + 4, :]
                act.activation(dst, bank[(0, 1, 6, 7)[n]][:, :].rearrange("p (a b) -> p a b", a=4), ACT.Copy)\
                    .then_inc(probT_ready, 1)
            for n in range(2):
                act.wait_ge(att_psum, n + 1)
                act.activation(mixT[:, 4 + 2 * n:6 + 2 * n, :], bank[n][:, :].rearrange("p (a b) -> p a b", a=2),
                               ACT.Copy).then_inc(att_ready, 1)
            for t in range(T):
                act.wait_ge(gla_psum, t + 1)
                act.activation(square[:, t * GROUP:(t + 1) * GROUP], bank[2 + t][:, :], ACT.Square)\
                    .then_inc(gla_squared, 1)
            act.wait_ge(gla_summed, 2)
            act.activation(stat[:, 120:128], stat[:, 112:120], ACT.Sqrt, bias=eps[:, 0:1], scale=1.0 / GDV)\
                .then_inc(gla_root, 1)
            for n in range(2):
                act.wait_ge(glaT_psum, n + 1)
                act.activation(mixT[:, 2 * n:2 * n + 2, :], bank[4 + n][:, :].rearrange("p (a b) -> p a b", a=2),
                               ACT.Copy, scale=gains[:, GN:GN + 1]).then_inc(glaT_ready, 1)
            for t in range(T):
                act.wait_ge(x1_ready, (2, 4)[t])
                act.activation(squares2, acc[:, t, :], ACT.Square, accum_out=stat[:, t:t + 1]).then_inc(sq2, 1)
                act.wait_ge(sq2, t + 1)
                act.activation(stat[:, 2 + t:3 + t], stat[:, t:t + 1], ACT.Sqrt, bias=eps[:, 0:1], scale=1.0 / D)\
                    .then_inc(root2, 1)
                act.wait_ge(x1T_psum, 2 * t + 1)
                act.activation(x1T[:, 0:4, t * P:(t + 1) * P], bank[2 + 2 * t][:, :].rearrange("p (a b) -> p a b", a=4),
                               ACT.Copy).then_inc(x1T_act, 1)
                act.wait_ge(rstd2, t + 1)
                act.activation(h2_parts[0][:, t, :], acc[:, t, :], ACT.Copy, scale=stat[:, t:t + 1])\
                    .then_inc(part0_ready, 1)
                act.wait_ge(rest_ready, t + 1)
                act.activation(h2_parts[1][:, t, :], h2_rest, ACT.Copy).then_inc(part1_ready, 1)
            for t in range(T):
                act.wait_ge(top_ready, t + 1)
                act.activation(top_exp[:, t, :], top_val[:, t, 0:TOPK], ACT.Exp, bias=stat[:, 4 + t:5 + t])\
                    .then_inc(top_expd, 1)

            def run(it, quad, rnd):
                for a in range(PAIRS):
                    j = it * PAIRS + a
                    for hf in range(2):
                        act.wait_ge(glu_clipped, 2 * j + hf + 1)
                        act.activation(sig[:, hf, :], glu_c[:, hf, :], ACT.Sigmoid, scale=ALPHA)\
                            .then_inc(sig_ready, 1)
                    for hf in range(2):
                        act.wait_ge(hiddenT_psum, 2 * j + hf + 1)
                        act.activation(actT[:, 4 * hf:4 * hf + 4, :],
                                       bank[4 + hf][:, :].rearrange("p (a b) -> p a b", a=4), ACT.Copy)\
                            .then_inc(hiddenT_ready, 1)
                    act.wait_ge(gatherT_psum, j + 1)
                    act.activation(gatherT, bank[0][:, 0:S], ACT.Copy).then_inc(gatherT_ready, 1)
                    for dh in range(2):
                        act.wait_ge(y_psum, 2 * j + dh + 1)
                        act.activation(y_sb[:, dh, :], bank[6 + dh][:, :], ACT.Copy).then_inc(y_ready, 1)

            all_rounds(act, run)

        @block.vector
        def _(dve):
            steps = [0]

            def step(ins):
                steps[0] += 1
                ins.then_inc(vec_step, 1)
                dve.wait_ge(vec_step, steps[0])

            dve.wait_ge(g1_turned, 1)
            dve.tensor_copy(gains[:, 0:KD], bank[6][:, 0:KD]).then_inc(g1_ready, 1)
            dve.wait_ge(g1_ready, 1)
            for t in range(T):
                for n in range(2):
                    dve.wait_ge(hT_psum, 2 * t + n + 1)
                    g = gains[:, G1 + 4 * n:G1 + 4 * n + 4].unsqueeze(2)
                    dve.tensor_tensor(hT[:, 4 * n:4 * n + 4, t * P:(t + 1) * P],
                                      bank[2 * t + n][:, :].rearrange("p (c s) -> p c s", c=4),
                                      g.to_broadcast([P, 4, P]), ALU.mult).then_inc(hT_ready, 1)
            dve.wait_ge(root1, 1)
            dve.reciprocal(stat[:, 0:2], stat[:, 2:4]).then_inc(rstd1, 1)
            dve.wait_ge(params_turned, 1)
            dve.tensor_copy(gains[:, KD:], bank[7][:, KD:19]).then_inc(gains_ready, 1)

            def normalise(g):
                for t in range(T):
                    dve.wait_ge(qk_squared, 2 * g + t + 1)
                    dve.tensor_reduce(stat[:, 64 + 16 * g + 8 * t:72 + 16 * g + 8 * t],
                                      square[:, t * GROUP:(t + 1) * GROUP].rearrange("p (h d) -> p h d", h=AH),
                                      AX, ALU.add).then_inc(qk_summed, 1)
                dve.wait_ge(qk_root, g + 1)
                r = stat[:, 32 + 16 * g:48 + 16 * g]
                step(dve.reciprocal(r, r))
                for t in range(T):
                    v = proj[:, t, g * GROUP:(g + 1) * GROUP].rearrange("p (h d) -> p h d", h=AH)
                    rs = stat[:, 32 + 16 * g + 8 * t:40 + 16 * g + 8 * t].unsqueeze(2)
                    dve.tensor_tensor(v, v, rs.to_broadcast([P, AH, ADH]), ALU.mult).then_inc(qk_normed, 1)

            normalise(0)
            normalise(1)
            dve.wait_ge(bias_in, 96)
            step(dve.tensor_copy(bias_parts[0:96, :], bias_raw[0:96, :]))
            step(dve.tensor_tensor(bias_rest[0:96, :], bias_raw[0:96, :], bias_parts[0:96, :], ALU.subtract))
            step(dve.tensor_copy(bias_parts[32:64, :], bias_rest[32:64, :]))
            step(dve.tensor_copy(bias_parts[64:96, :], bias_rest[64:96, :]))
            step(dve.tensor_tensor(bias_rest[64:96, :], bias_rest[64:96, :], bias_parts[64:96, :], ALU.subtract))
            dve.tensor_copy(bias_parts[64:96, :], bias_rest[64:96, :]).then_inc(bias_split, 1)
            dve.wait_ge(small_in, 80)
            dve.tensor_tensor(w_router[:, :, :], w_router[:, :, :],
                              gains[:, G2:G2 + KD].unsqueeze(2).to_broadcast([P, KD, NE]), ALU.mult)\
                .then_inc(router_scaled, 1)
            dve.wait_ge(rel_in, 32)
            for t in range(T):
                step(dve.memset(rel[t][0:CHUNK, :, 0:CHUNK], MASK_VALUE))

            def add_bias(t):
                if t == 0:
                    for b in range(2):
                        dve.wait_ge(score_psum, b + 1)
                        dve.scalar_tensor_tensor(scores[0][:, b::2, :], bank[b][:, :].rearrange("p (a k) -> p a k", a=4),
                                                 ADH ** -0.5, rel[0][:, b::2, ::-1], ALU.mult, ALU.add)\
                            .then_inc(score_ready, 1)
                else:
                    for n in range(4):
                        b, half = n % 2, n // 2
                        dve.wait_ge(score_psum, 3 + n)
                        dve.scalar_tensor_tensor(scores[1][:, 4 * half + b:4 * half + b + 3:2, :],
                                                 bank[n][:, :].rearrange("p (a k) -> p a k", a=2),
                                                 ADH ** -0.5, rel[1][:, 4 * half + b:4 * half + b + 3:2, ::-1],
                                                 ALU.mult, ALU.add).then_inc(score_ready, 1)
                dve.wait_ge(score_ready, (2, 6)[t])
                m = stat[:, 8 + 8 * t:16 + 8 * t]
                step(dve.tensor_reduce(m, scores[t], AX, ALU.max))
                dve.tensor_scalar(m, m, -1.0, None, ALU.mult).then_inc(max_ready, 1)

            def scale_probs(t):
                dve.wait_ge(exp_ready, t + 1)
                r = stat[:, 96 + 8 * t:104 + 8 * t]
                step(dve.reciprocal(r, r))
                dve.tensor_tensor(scores[t], scores[t], r.unsqueeze(2).to_broadcast([P, AH, P * (t + 1)]), ALU.mult)\
                    .then_inc(prob_ready, 1)

            add_bias(0)
            scale_probs(0)
            dve.wait_ge(abs_z, 3)
            dve.scalar_tensor_tensor(log_a, bank[2][:, :].rearrange("p (t n) -> p t n", t=T), 0.0, decay_tok,
                                     ALU.min, ALU.subtract).then_inc(log_ready, 1)
            add_bias(1)
            dve.wait_ge(rev_exp, 1)
            dve.tensor_tensor(k_dec, proj[:, :, GQK * GROUP + 256:GQK * GROUP + 512], decay_tok, ALU.mult)\
                .then_inc(kdec_ready, 1)
            scale_probs(1)
            dve.wait_ge(u_psum, 4)
            dve.wait_ge(rev_exp, 2)
            for n in range(NCH):
                t, c = divmod(n, 2)
                ub = bank[2 + 2 * c + t]
                for pr in range(2):
                    for b in range(2):
                        rows, cols = slice(64 * b, 64 * b + 64), slice(P * b, P * b + P)
                        u = ub[rows, pr * S + P * b:pr * S + P * b + P]
                        if n == 0:
                            ins = dve.tensor_copy(state[rows, n, pr, cols], u)
                        else:
                            ins = dve.scalar_tensor_tensor(state[rows, n, pr, cols], state[rows, n - 1, pr, cols],
                                                           stat[rows, 24 + 4 * pr + n:25 + 4 * pr + n], u,
                                                           ALU.mult, ALU.add)
                ins.then_inc(state_ready, 1)
                dve.wait_ge(state_ready, n + 1)
            dve.wait_ge(gate_sig, 1)
            step(dve.tensor_tensor(out_gate, out_gate, proj[:, :, 5 * GROUP:6 * GROUP], ALU.mult))
            for t in range(T):
                dve.wait_ge(gla_squared, t + 1)
                dve.tensor_reduce(stat[:, 112 + 4 * t:116 + 4 * t],
                                  square[:, t * GROUP:(t + 1) * GROUP].rearrange("p (h d) -> p h d", h=GH),
                                  AX, ALU.add).then_inc(gla_summed, 1)
            dve.wait_ge(gla_root, 1)
            step(dve.reciprocal(stat[:, 120:128], stat[:, 120:128]))
            for t in range(T):
                for h in range(GH):
                    cols = slice(h * GDV, (h + 1) * GDV)
                    ins = dve.scalar_tensor_tensor(gla_o[:, t, cols], bank[2 + t][:, cols],
                                                   stat[:, 120 + 4 * t + h:121 + 4 * t + h],
                                                   out_gate[:, t, cols], ALU.mult, ALU.mult)
                ins.then_inc(gla_normed, 1)

            def residual(t, dh):
                dve.wait_ge(mix_psum, 2 * t + dh + 1)
                v = acc[:, t, dh * GROUP:(dh + 1) * GROUP]
                dve.tensor_tensor(v, bank[(6, 7, 0, 1)[2 * t + dh]][:, :], v, ALU.add).then_inc(x1_ready, 1)

            def x1_turned(t):
                dve.wait_ge(x1T_psum, 2 * t + 2)
                dve.tensor_copy(x1T[:, 4:8, t * P:(t + 1) * P], bank[3 + 2 * t][:, :].rearrange("p (a b) -> p a b", a=4))\
                    .then_inc(x1T_dve, 1)

            def rms(t):
                dve.wait_ge(root2, t + 1)
                dve.reciprocal(stat[:, t:t + 1], stat[:, 2 + t:3 + t]).then_inc(rstd2, 1)

            def split_rest(t):
                dve.wait_ge(part0_ready, t + 1)
                dve.scalar_tensor_tensor(h2_rest, acc[:, t, :], stat[:, t:t + 1], h2_parts[0][:, t, :],
                                         ALU.mult, ALU.subtract).then_inc(rest_ready, 1)

            def split_last(t):
                dve.wait_ge(part1_ready, t + 1)
                dve.tensor_tensor(h2_parts[2][:, t, :], h2_rest, h2_parts[1][:, t, :], ALU.subtract)\
                    .then_inc(h2_ready, 1)

            def choose(t):
                dve.wait_ge(logit_psum, t + 1)
                logit = route_tmp[:, t, :]
                step(dve.scalar_tensor_tensor(logit, bank[6 + t][:, 0:NE], stat[:, t:t + 1], b_router[:, :],
                                              ALU.mult, ALU.add))
                step(dve.max(top_val[:, t, :], logit))
                step(dve.max_index(top_idx[:, t, :], top_val[:, t, :], logit))
                dve.tensor_scalar(stat[:, 4 + t:5 + t], top_val[:, t, 0:1], -1.0, None, ALU.mult).then_inc(top_ready, 1)
                step(dve.tensor_copy(top_idx_f[:, t, :], top_idx[:, t, :]))
                step(dve.tensor_tensor(onehot[:, TOPK * t:TOPK * (t + 1), :],
                                       expert_iota[:, :].unsqueeze(1).to_broadcast([P, TOPK, NE]),
                                       top_idx_f[:, t, 0:TOPK].unsqueeze(2).to_broadcast([P, TOPK, NE]),
                                       ALU.is_equal))
                dve.tensor_reduce(mask[:, t, :], onehot[:, TOPK * t:TOPK * (t + 1), :].rearrange("p k e -> p e k"),
                                  AX, ALU.add).then_inc(mask_ready, 1)

            def pick_biases(a, quad):
                dve.tensor_scalar(bias_pick[a], expert_diff[:, :], pair_first[:, bass.ds(quad * PAIRS + a, 1)], None,
                                  ALU.is_equal).then_inc(bias_pick_ready, 1)

            residual(0, 0)
            residual(0, 1)
            residual(1, 0)
            x1_turned(0)
            rms(0)
            split_rest(0)
            residual(1, 1)
            split_last(0)
            x1_turned(1)
            rms(1)
            choose(0)
            split_rest(1)
            choose(1)
            pick_biases(0, 0)
            dve.wait_ge(top_expd, 2)
            step(dve.tensor_reduce(stat[:, 4:6], top_exp[:, :, :], AX, ALU.add))
            step(dve.reciprocal(stat[:, 4:6], stat[:, 4:6]))
            step(dve.tensor_tensor(top_exp[:, :, :], top_exp[:, :, :],
                                   stat[:, 4:6].unsqueeze(2).to_broadcast([P, T, TOPK]), ALU.mult))
            for t in range(T):
                ins = dve.tensor_tensor(gated_hot[:, TOPK * t:TOPK * (t + 1), :], onehot[:, TOPK * t:TOPK * (t + 1), :],
                                        top_exp[:, t, :].unsqueeze(2).to_broadcast([P, TOPK, NE]), ALU.mult)
            step(ins)
            for t in range(T):
                dve.tensor_reduce(gates[:, t, :], gated_hot[:, TOPK * t:TOPK * (t + 1), :].rearrange("p k e -> p e k"),
                                  AX, ALU.add)
            dve.wait_ge(rank_psum, 1)
            rank = route_tmp
            step(dve.scalar_tensor_tensor(rank, bank[4][:, 0:T * NE].rearrange("p (t e) -> p t e", t=T), 1.0,
                                          mask[:, :, :], ALU.add, ALU.mult))
            for r in range(ROUNDS):
                ins = dve.tensor_scalar(slot_of[:, :, r, :], rank, -1.0 - SLOTS * r, None, ALU.add)
            ins.then_inc(slots_ready, 1)
            dve.wait_ge(slots_ready, 1)

            def find_rounds():
                step(dve.tensor_reduce(counts[0:1, 32:40], bank[5][0:1, 0:NE].rearrange("p (q e) -> p q e", e=EPI),
                                       AX, ALU.max))
                for r in range(1, ROUNDS):
                    dve.tensor_scalar(flags[0:1, flag_column(0, r):flag_column(0, r) + ITERS], counts[0:1, 32:40],
                                      float(SLOTS * r), None, ALU.is_gt)
                step(dve.tensor_reduce(counts[0:1, 40:41], counts[0:1, 32:40], AX, ALU.max))
                dve.tensor_scalar(flags[0:1, 24:25], counts[0:1, 40:41], float(SLOTS), None, ALU.is_gt)\
                    .then_inc(flags_ready, 1)

            def route(j, a, quad, rnd, gated):
                for e in range(2):
                    for t in range(T):
                        n = quad * EPI + 2 * a + e
                        at = slot_of[:, t, rnd, bass.ds(n, 1)]
                        if gated:
                            ins = dve.tensor_scalar(pick_gated[a][:, t, e * SLOTS:(e + 1) * SLOTS], slot_iota[:, :],
                                                    at, gates[:, t, bass.ds(n, 1)], ALU.is_equal, ALU.mult)
                        else:
                            ins = dve.tensor_scalar(pick[a][:, t, e * SLOTS:(e + 1) * SLOTS], slot_iota[:, :],
                                                    at, None, ALU.is_equal)
                ins.then_inc(gated_ready if gated else route_ready, 1)

            def packed(j, a):
                for n in range(2):
                    dve.wait_ge(pack_psum, 2 * j + n + 1)
                    g = gains[:, G2 + 4 * n:G2 + 4 * n + 4].unsqueeze(2)
                    dve.tensor_tensor(xeT[a][:, 4 * n:4 * n + 4, :], bank[6 + n][:, :].rearrange("p (c s) -> p c s", c=4),
                                      g.to_broadcast([P, 4, P]), ALU.mult).then_inc(pack_ready, 1)

            def hidden(j):
                for hf in range(2):
                    dve.wait_ge(hidden_psum, 4 * j + 2 * hf + 1)
                    dve.tensor_scalar(glu_c[:, hf, :], bank[hf][:, :], LIMIT, None, ALU.min).then_inc(glu_clipped, 1)
                    dve.wait_ge(hidden_psum, 4 * j + 2 * hf + 2)
                    dve.tensor_scalar(lin_c[:, hf, :], bank[2 + hf][:, :], LIMIT, -LIMIT, ALU.min, ALU.max)\
                        .then_inc(lin_clipped, 1)
                for hf in range(2):
                    dve.wait_ge(sig_ready, 2 * j + hf + 1)
                    dve.tensor_tensor(sig[:, hf, :], glu_c[:, hf, :], sig[:, hf, :], ALU.mult).then_inc(glu_ready, 1)
                    dve.wait_ge(glu_ready, 2 * j + hf + 1)
                    dve.scalar_tensor_tensor(act_t[:, hf, :], lin_c[:, hf, :], 1.0, sig[:, hf, :], ALU.add, ALU.mult)\
                        .then_inc(hidden_ready, 1)

            def combine(j):
                for n in range(4):
                    dh, t = divmod(n, 2)
                    dve.wait_ge(comb_psum, 3 * j + max(n, 1))
                    v = acc[:, t, dh * GROUP:(dh + 1) * GROUP]
                    dve.tensor_tensor(v, bank[4 + n][:, :], v, ALU.add).then_inc(comb_added, 1)

            def run(it, quad, rnd):
                j = it * PAIRS
                first = isinstance(it, int)
                if not first:
                    dve.wait_ge(comb_psum, 3 * j)
                    pick_biases(0, quad)
                route(j, 0, quad, rnd, False)
                if first:
                    split_last(1)
                    find_rounds()
                pick_biases(1, quad)
                route(j + 1, 1, quad, rnd, False)
                route(j, 0, quad, rnd, True)
                route(j + 1, 1, quad, rnd, True)
                packed(j, 0)
                hidden(j)
                packed(j + 1, 1)
                combine(j)
                hidden(j + 1)
                combine(j + 1)

            all_rounds(dve, run)
            dve.drain().then_inc(result_ready, 1)

        @block.tensor
        def _(pe):
            pe.wait_ge(ident_ready, 1)
            pe.wait_ge(g1_in, 16)
            pe.transpose(bank[6][:, 0:KD], params[0:KD, :], ident[0:KD, 0:KD]).then_inc(g1_turned, 1)
            for t in range(T):
                pe.wait_ge(x_in[t], 16)
                for k in range(KD):
                    ins = pe.transpose(bank[2 * t + k // 4][:, (k % 4) * P:(k % 4 + 1) * P],
                                       acc[:, t, k * P:(k + 1) * P], ident[:, :])
                    if k % 4 == 3:
                        ins.then_inc(hT_psum, 1)

            def project(g, tiles=(0, 1)):
                if g >= 2:
                    pe.wait_ge(proj_ready, 2 * (g - 1))
                if g == 1:
                    pe.wait_ge(gains_ready, 1)
                if g > 0:
                    pe.wait_ge(w_in_full[g], 16)
                for t in tiles:
                    for k in range(KD):
                        if g == 0:
                            pe.wait_ge(hT_ready, 2 * t + k // 4 + 1)
                            pe.wait_ge(w_first_full[k // 2], 16)
                        ins = pe.matmul(bank[4 + 2 * (g % 2) + t][:, :], hT[:, k, t * P:(t + 1) * P],
                                        w_buf[g][:, k, :], start=(k == 0), stop=(k == KD - 1))
                    ins.then_inc(proj_psum, 1)

            project(AQ)
            pe.wait_ge(params_in, 16 * 6)
            pe.transpose(bank[7][:, 0:19], params[0:19, :], ident[0:19, 0:19]).then_inc(params_turned, 1)
            project(AK)
            pe.wait_ge(small_in, 80)
            for t in range(T):
                for k in range(KD):
                    ins = pe.matmul(bank[0][:, t * GRANK:(t + 1) * GRANK], hT[:, k, t * P:(t + 1) * P], w_lr[:, k, :],
                                    start=(k == 0), stop=(k == KD - 1))
            ins.then_inc(lr_psum, 1)
            project(AV, (0,))
            pe.wait_ge(low_rank_ready, 2)
            for t in range(T):
                ins = pe.transpose(bank[1][0:GRANK, t * P:(t + 1) * P], low_rank[:, t, :], ident[:, :])
            ins.then_inc(lrT_psum, 1)
            project(AV, (1,))
            pe.wait_ge(lr_ready, 1)
            for g in range(2):
                pe.wait_ge(qk_normed, 2 * g + 2)
                for pr in range(4):
                    for t in range(T):
                        ins = pe.transpose(bank[2 * g + pr // 2][:, (pr % 2) * S + t * P:(pr % 2) * S + (t + 1) * P],
                                           proj[:, t, g * GROUP + pr * P:g * GROUP + (pr + 1) * P], ident[:, :])
                    if pr % 2:
                        ins.then_inc(qkT_psum, 1)
            project(GQK)

            def score(t):
                keys = P * (t + 1)
                if t == 0:
                    pe.wait_ge(qkT_ready, 4)
                else:
                    pe.wait_ge(score_ready, 2)
                    pe.wait_ge(log_ready, 1)
                    pe.wait_ge(glaq_ready, 1)
                for half in range(1 if t == 0 else 2):
                    width = 4 if t == 0 else 2
                    for i in range(width):
                        pr = half * width + i
                        for b in range(2):
                            rows = slice(64 * b, 64 * b + 64)
                            ins = pe.matmul(bank[2 * half + b][:, i * keys:(i + 1) * keys],
                                            att_qT[rows, pr, t * P:(t + 1) * P], att_kT[rows, pr, 0:keys],
                                            start=True, stop=True)
                            if i == width - 1:
                                ins.then_inc(score_psum, 1)

            score(0)
            for t in range(T):
                ins = pe.matmul(bank[2][:, t * S:(t + 1) * S], lrT[0:GRANK + 1, t * P:(t + 1) * P], gate_up,
                                start=True, stop=True)
            ins.then_inc(z_psum, 1)
            pe.wait_ge(proj_ready, 2 * GQK + 2)
            for pr in range(2):
                for t in range(T):
                    c = GQK * GROUP + pr * P
                    ins = pe.transpose(bank[3][:, pr * S + t * P:pr * S + (t + 1) * P], proj[:, t, c:c + P], ident[:, :])
            ins.then_inc(glaq_psum, 1)
            project(GV)
            score(1)
            project(OG, (0,))
            pe.wait_ge(proj_ready, 10)
            for t in range(T):
                ins = pe.matmul(bank[4][:, t * S:(t + 1) * S], later[:, :], log_a[:, t, :], start=True, stop=True)
            ins.then_inc(rev_psum, 1)
            for pr in range(2):
                for t in range(T):
                    ins = pe.matmul(bank[5][:, 4 * pr + 2 * t:4 * pr + 2 * t + 2], log_a[:, t, pr * P:(pr + 1) * P],
                                    chunk_of[:, :], start=True, stop=True)
            ins.then_inc(rev_psum, 1)
            pe.wait_ge(prob_ready, 1)
            pe.wait_ge(score_ready, 6)
            for h in range(AH):
                ins = pe.transpose(bank[h // 4][:, (h % 4) * P:(h % 4 + 1) * P], scores[0][:, h, :], ident[:, :])
                if h % 4 == 3:
                    ins.then_inc(probT_psum, 1)
            project(OG, (1,))
            pe.wait_ge(kdec_ready, 1)
            pe.wait_ge(rev_exp, 2)
            for t in range(T):
                for pr in range(2):
                    for c in range(2):
                        rows = slice(64 * c, 64 * c + 64)
                        col = GV * GROUP + pr * S
                        ins = pe.matmul(bank[2 + 2 * c + t][:, pr * S:(pr + 1) * S], k_dec[rows, t, pr * P:(pr + 1) * P],
                                        proj[rows, t, col:col + S], start=True, stop=True)
                        if pr:
                            ins.then_inc(u_psum, 1)
            pe.wait_ge(prob_ready, 2)
            pe.wait_ge(probT_ready, 2)
            pe.wait_ge(proj_ready, 12)
            for kt in range(2):
                for h in range(AH):
                    ins = pe.transpose(bank[6 * kt + h // 4][:, (h % 4) * P:(h % 4 + 1) * P],
                                       scores[1][:, h, kt * P:(kt + 1) * P], ident[:, :])
                    if h % 4 == 3:
                        ins.then_inc(probT_psum, 1)
            pe.wait_ge(probT_ready, 6)
            for pr in range(4):
                for b in range(2):
                    h = 2 * pr + b
                    o_ = bank[pr // 2][64 * b:64 * b + 64, (pr % 2) * S:(pr % 2) * S + S]
                    vc = AV * GROUP + h * ADH
                    pe.matmul(o_, proj[:, 0, vc:vc + ADH], probT[0][:, h, :], start=True, stop=False)
                    ins = pe.matmul(o_[:, P:S], proj[:, 1, vc:vc + ADH], probT[1][:, h, :], start=False, stop=True)
                if pr % 2:
                    ins.then_inc(att_psum, 1)
            for n in range(NCH):
                t, c = divmod(n, 2)
                pe.wait_ge(state_ready, 4 if n == 0 else n + 1)
                for pr in range(2):
                    ins = pe.matmul(bank[2 + t][64 * c:64 * c + 64, pr * S:(pr + 1) * S],
                                    gla_qT[:, pr, n * CHUNK:(n + 1) * CHUNK], state[:, n, pr, :], start=True, stop=True)
                if c:
                    ins.then_inc(gla_psum, 1)

            def mix(t, first_k, cols=(0, 1)):
                for dh in cols:
                    for k in range(first_k, first_k + 4):
                        ins = pe.matmul(bank[(6, 7, 0, 1)[2 * t + dh]][:, :], mixT[:, k, t * P:(t + 1) * P],
                                        w_out_sb[:, k, dh * GROUP:(dh + 1) * GROUP], start=(k == 4), stop=(k == 3))
                    if first_k == 0:
                        ins.then_inc(mix_psum, 1)

            def turn_x1(t, half):
                pe.wait_ge(x1_ready, 2 * t + half + 1)
                for k in range(4 * half, 4 * half + 4):
                    ins = pe.transpose(bank[2 + 2 * t + half][:, (k % 4) * P:(k % 4 + 1) * P],
                                       acc[:, t, k * P:(k + 1) * P], ident[:, :])
                ins.then_inc(x1T_psum, 1)

            def logits(t):
                pe.wait_ge(x1T_act, t + 1)
                for k in range(KD):
                    if k == 4:
                        pe.wait_ge(x1T_dve, t + 1)
                    ins = pe.matmul(bank[6 + t][:, 0:NE], x1T[:, k, t * P:(t + 1) * P], w_router[:, k, :],
                                    start=(k == 0), stop=(k == KD - 1))
                ins.then_inc(logit_psum, 1)

            pe.wait_ge(w_out_full[0], 16)
            pe.wait_ge(w_out_full[1], 16)
            pe.wait_ge(att_ready, 2)
            pe.wait_ge(probT_ready, 6)
            mix(0, 4)
            pe.wait_ge(gla_normed, 2)
            for h in range(GH):
                for t in range(T):
                    ins = pe.transpose(bank[4 + h // 2][:, (h % 2) * S + t * P:(h % 2) * S + (t + 1) * P],
                                       gla_o[:, t, h * GDV:(h + 1) * GDV], ident[:, :])
                if h % 2:
                    ins.then_inc(glaT_psum, 1)
            mix(1, 4)
            pe.wait_ge(glaT_ready, 2)
            mix(0, 0)
            mix(1, 0, (0,))
            turn_x1(0, 0)
            turn_x1(0, 1)
            mix(1, 0, (1,))
            turn_x1(1, 0)
            pe.wait_ge(router_scaled, 1)
            logits(0)
            turn_x1(1, 1)
            logits(1)
            pe.wait_ge(mask_ready, 2)
            pe.matmul(bank[5][0:1, 0:NE], ones[:, 0:1], mask[:, 0, :], start=True, stop=False)
            pe.matmul(bank[5][0:1, 0:NE], ones[:, 0:1], mask[:, 1, :], start=False, stop=True)
            pe.matmul(bank[4][:, 0:NE], before[:, :], mask[:, 0, :], start=True, stop=True)
            pe.matmul(bank[4][:, NE:2 * NE], ones[:, :], mask[:, 0, :], start=True, stop=False)
            pe.matmul(bank[4][:, NE:2 * NE], before[:, :], mask[:, 1, :], start=False, stop=True).then_inc(rank_psum, 1)

            def pack(j, a, first, halves=(0, 1)):
                pe.wait_ge(route_ready, j + 1)
                if first:
                    pe.wait_ge(h2_ready, 2)
                elif a == 0:
                    pe.wait_ge(comb_added, 4 * j)
                for c in range(4 * halves[0], 4 * halves[-1] + 4):
                    for t in range(T):
                        for i in range(3):
                            ins = pe.matmul(bank[6 + c // 4][:, (c % 4) * P:(c % 4 + 1) * P],
                                            h2_parts[i][:, t, c * P:(c + 1) * P], pick[a][:, t, :],
                                            start=(t == 0 and i == 0), stop=(t == T - 1 and i == 2))
                            if a == 1 and c == 0 and t == 0 and i == 0:
                                ins.then_inc(chunks_used, 1)
                    if c % 4 == 3:
                        ins.then_inc(pack_psum, 1)

            def chunk(c, first):
                return extra[c - FIRST_EXTRA] if first and FIRST_EXTRA <= c < RING else ring[:, c % RING, :]

            def arrived(it, c, first):
                if first and FIRST_EXTRA <= c < RING:
                    pe.wait_ge(extra_full[c - FIRST_EXTRA], 16)
                    return
                fills = c // RING + (1 if c % RING < FIRST_EXTRA else 0)
                pe.wait_ge(ring_full[c % RING], it * (16 * (ITER_CHUNKS // RING)) + 16 * fills)

            def hidden_bias(j, a, first):
                pe.wait_ge(bias_pick_ready, j + 1)
                if first:
                    pe.wait_ge(bias_split, 1)
                    pe.wait_ge(x1_ready, 4)
                    pe.wait_ge(x1T_act, 1)
                    pe.wait_ge(x1T_dve, 1)
                else:
                    pe.wait_ge(hidden_ready, 2 * j)
                    pe.wait_ge(gatherT_ready, j)
                for n in range(4):
                    pe.matmul(bank[n][:, :], bias_pick[a], bias_parts[:, n * GROUP:(n + 1) * GROUP],
                              start=True, stop=False, skip_group_check=True)

            def up(it, j, a, first):
                hidden_bias(j, a, first)
                if first:
                    pack(j, 0, True, (0,))
                for k in range(KD):
                    if first and k == KD // 2:
                        pack(j, 0, True, (1,))
                    if k % (KD // 2) == 0:
                        pe.wait_ge(pack_ready, 2 * j + 1 + 2 * k // KD)
                    c = a * JOB_CHUNKS + 2 * k
                    arrived(it, c, first)
                    arrived(it, c + 1, first)
                    for n in (0, 2, 1, 3):
                        for e in range(2):
                            ins = pe.matmul(bank[n][64 * e:64 * e + 64, :], xeT[a][:, k, 64 * e:64 * e + 64],
                                            chunk(c + e, first)[:, n * GROUP:(n + 1) * GROUP],
                                            start=False, stop=(k == KD - 1), skip_group_check=True)
                            if n == 3 and (e == 0 or k < KD - 1):
                                ins.then_inc(chunks_used, 1)
                        if k == KD - 1:
                            ins.then_inc(hidden_psum, 1)

            def turn(j, a, first):
                if not first:
                    pe.wait_ge(comb_added, 4 * j)
                for hf in range(2):
                    pe.wait_ge(hidden_ready, 2 * j + hf + 1)
                    for i in range(4):
                        ins = pe.transpose(bank[4 + hf][:, i * P:(i + 1) * P], act_t[:, hf, i * P:(i + 1) * P], ident[:, :])
                        if a == 1 and hf == 0 and i == 0:
                            ins.then_inc(chunks_used, 1)
                    ins.then_inc(hiddenT_psum, 1)
                pe.wait_ge(gated_ready, j + 1)
                for t in range(T):
                    ins = pe.transpose(bank[0][:, t * P:(t + 1) * P], pick_gated[a][:, t, :], ident[:, :])
                ins.then_inc(gatherT_psum, 1)

            def down(it, j, a, first):
                pe.wait_ge(pack_ready, 2 * j + 4 if a == 0 else 2 * j + 2)
                pe.wait_ge(hiddenT_ready, 2 * j + 2)
                for dh in range(2):
                    c0 = 2 * D + dh * GROUP
                    pe.matmul(bank[6 + dh][:, :], bias_pick[a], bias_parts[:, c0:c0 + GROUP],
                              start=True, stop=False, skip_group_check=True)
                for i in range(KD // 2):
                    c = a * JOB_CHUNKS + 2 * KD + 2 * i
                    arrived(it, c, False)
                    arrived(it, c + 1, False)
                    last = i == KD // 2 - 1
                    for kk, dh in ((0, 0), (1, 0), (0, 1), (1, 1)) if last else ((0, 0), (0, 1), (1, 0), (1, 1)):
                        for e in range(2):
                            f = kk * D + dh * GROUP
                            ins = pe.matmul(bank[6 + dh][64 * e:64 * e + 64, :],
                                            actT[:, 2 * i + kk, 64 * e:64 * e + 64],
                                            ring[:, (c + e) % RING, f:f + GROUP], start=False, stop=last and kk == 1,
                                            skip_group_check=True)
                            if kk == 1 and dh == 1 and (e == 0 or not last):
                                ins.then_inc(chunks_used, 1)
                        if last and kk == 1:
                            ins.then_inc(y_psum, 1)

            def spread(j):
                pe.wait_ge(gatherT_ready, j + 1)
                for n in range(4):
                    dh, t = divmod(n, 2)
                    pe.wait_ge(y_ready, 2 * j + 1 + dh)
                    ins = pe.matmul(bank[4 + n][:, :], gatherT[:, t * P:(t + 1) * P], y_sb[:, dh, :],
                                    start=True, stop=True)
                    ins.then_inc(comb_psum if n else chunks_used, 1)

            def run(it, quad, rnd):
                first = isinstance(it, int)
                j = it * PAIRS
                if not first:
                    pack(j, 0, False)
                up(it, j, 0, first)
                pack(j + 1, 1, False)
                turn(j, 0, first)
                down(it, j, 0, first)
                spread(j)
                up(it, j + 1, 1, False)
                turn(j + 1, 1, False)
                down(it, j + 1, 1, False)
                spread(j + 1)

            all_rounds(pe, run)


_INS = ['x', 'norm1_g', 'w_in', 'gla_gate_up', 'gla_gate_bias', 'gla_norm_g', 'q_norm_g', 'k_norm_g',
        'rel_bias', 'w_out', 'norm2_g', 'router_w', 'router_b', 'moe_w_in', 'moe_b_in', 'moe_w_out', 'moe_b_out']
_OUTS = [((1, S, D), 'float32')]


def kernel(**inputs):
    import numpy as _np
    import concourse.bacc as _bacc
    from concourse import mybir as _mybir
    from concourse.bass_utils import run_bass_kernel_spmd as _run

    nc = _bacc.Bacc("TRN2", target_bir_lowering=False, num_devices=1)
    arrays, args = {}, []
    for name in _INS:
        a = _np.ascontiguousarray(inputs[name])
        arrays[f"in_{name}_dram"] = a
        args.append(nc.dram_tensor(f"in_{name}_dram", a.shape, _mybir.dt.from_np(a.dtype), kind="ExternalInput").ap())
    for i, (shape, dtype) in enumerate(_OUTS):
        dt = _mybir.dt.from_np(_np.dtype(dtype))
        args.append(nc.dram_tensor(f"out_{i}_dram", shape, dt, kind="ExternalOutput").ap())
    build(nc, *args)
    r = _run(nc, [arrays], core_ids=[0])
    return r.results[0]["out_0_dram"]
```

```python
from contextlib import ExitStack

import concourse.bass as bass
from concourse import mybir

P = 128
D = 1024
S = 256
T = S // P
CHUNK = 64
NCH = S // CHUNK
KD = D // P
EPS = 1e-6
GH, GDK, GDV, GRANK, GTAU = 4, 64, 128, 16, 16.0
AH, ADH = 8, 64
REL_CLIP = 256
MASK_VALUE = -1e30
NE, TOPK, F = 32, 4, 1024
ALPHA, LIMIT = 1.702, 7.0
GROUP = 512
UNITS = 4
SPLITS = 3
AQ, AK, AV, GQK, GV, OG = range(6)
GROUP_COL = (1552, 2064, 2576, 0, 512, 1040)
LR_COL = 1024

SLOTS = 64
ROUNDS = S // SLOTS
PAIRS = 2
EPI = 2 * PAIRS
ITERS = NE // EPI
CHUNK_F = 2048
RING = 16
JOB_CHUNKS = 2 * KD + KD
ITER_CHUNKS = PAIRS * JOB_CHUNKS
EXTRA = 4
FIRST_EXTRA = RING - EXTRA

F32 = mybir.dt.float32
F32R = mybir.dt.float32r
BF16 = mybir.dt.bfloat16
I32 = mybir.dt.int32
U32 = mybir.dt.uint32
ALU = mybir.AluOpType
ACT = mybir.ActivationFunctionType
AX = mybir.AxisListType.X


def build(nc, x, norm1_g, w_in, gla_gate_up, gla_gate_bias, gla_norm_g, q_norm_g, k_norm_g,
          rel_bias, w_out, norm2_g, router_w, router_b, moe_w_in, moe_b_in, moe_w_out,
          moe_b_out, out):
    with ExitStack() as ctx:
        def sb(name, shape, dt=F32):
            return ctx.enter_context(nc.sbuf_tensor(name, shape, dt))

        def sem(name):
            return ctx.enter_context(nc.semaphore(name))

        with nc.sbuf_tensor("split_parts", [P, 5 * CHUNK_F], F32R) as split_parts:
            parts = split_parts[:, :]
        ring = sb("ring", [P, RING, CHUNK_F])
        acc = sb("acc", [P, T, D])
        area = sb("area", [P, 15104])
        bias_parts = sb("bias_parts", [P, 3 * D], BF16)
        ident = sb("ident", [P, P])
        later = sb("later", [P, P])
        before = sb("before", [P, P])
        ones = sb("ones", [P, P])
        chunk_of = sb("chunk_of", [P, 2])
        eps = sb("eps", [P, 1])
        slot_iota = sb("slot_iota", [P, SLOTS])
        expert_iota = sb("expert_iota", [P, NE])
        expert_diff = sb("expert_diff", [P, P])
        pair_first = sb("pair_first", [P, NE // 2])
        gains = sb("gains", [P, 19])
        w_router = sb("w_router", [P, KD, NE])
        b_router = sb("b_router", [P, NE])
        stat = sb("stat", [P, 128])
        gates = sb("gates", [P, T, NE])
        mask = sb("mask", [P, T, NE])
        slot_of = sb("slot_of", [P, T, ROUNDS, NE])
        top_val = sb("top_val", [P, T, 8])
        top_idx = sb("top_idx", [P, T, 8], U32)
        top_idx_f = sb("top_idx_f", [P, T, 8])
        top_exp = sb("top_exp", [P, T, TOPK])
        counts = sb("counts", [1, 64])
        flags = sb("flags", [1, 32], I32)

        def part(base, off, *dims):
            n = 1
            for d in dims:
                n *= d
            v = base[:, off:off + n]
            if len(dims) == 1:
                return v
            names = "abc"[:len(dims)]
            return v.rearrange("p (%s) -> p %s" % (" ".join(names), " ".join(names)),
                               **{c: d for c, d in zip(names, dims)})

        hT_high, hT_low = (part(parts, i * KD * S, KD, S) for i in range(2))
        w_high = [part(parts, 2 * KD * S + i * 2 * GROUP, 2, GROUP) for i in range(SPLITS)]
        w_low = [part(parts, 2 * KD * S + (SPLITS + i) * 2 * GROUP, 2, GROUP) for i in range(SPLITS)]

        hT = part(area, 0, KD, S)
        mixT = hT
        proj = part(area, 2048, T, 6 * GROUP)
        o = 8192
        gla_qT = part(area, o, 2, S)
        log_a = part(area, o + 512, T, S)
        decay_tok = part(area, o + 1024, T, S)
        k_dec = part(area, o + 1536, T, S)
        state = part(area, o + 2048, NCH, 2, S)
        x_squares = part(area, 2048, T, D)
        gla_o = part(area, o + 4096, T, GROUP)
        out_gate = part(area, o + 5120, T, GROUP)
        lrT = part(area, o + 6144, S)
        low_rank = part(area, o + 512, T, GRANK)
        w_lr = part(area, o + 6400, KD, GRANK)
        gate_up = area[0:GRANK + 1, o + 6528:o + 6784]
        params = part(area, o + 6784, P)
        spare = ring[:, :, :].rearrange("p s f -> p (s f)")
        A0 = 6 * CHUNK_F
        scores = [part(spare, A0, AH, P), part(spare, A0 + 1024, AH, S)]
        probT = [part(spare, A0 + 3072, AH, S), part(spare, A0 + 5120, AH, P)]
        rel = [part(spare, A0 + 6144, AH, P), part(spare, A0 + 7168, AH, S)]
        att_qT = part(spare, A0 + 9216, AH // 2, S)
        att_kT = part(spare, A0 + 10240, AH // 2, S)
        square = part(spare, A0 + 11264, 2 * GROUP)
        b_in_raw = part(spare, 5 * CHUNK_F, 2 * D)
        b_out_raw = part(area, o + 4096, D)
        bias_rest = part(area, o + 5120, D)
        w_buf = [part(spare, (12 + 2 * (g % 2)) * CHUNK_F, KD, GROUP) for g in range(6)]
        w_out_sb = part(spare, 12 * CHUNK_F, KD, D)
        extra = [part(area, at, CHUNK_F) for at in (2048, 0, 11264, 9216)]
        glu_c = part(area, 0, 2, GROUP)
        sig = part(area, 1024, 2, GROUP)
        lin_c = part(area, 2048, 2, GROUP)
        act_t = part(area, 3072, 2, GROUP)
        h2_parts = [part(area, 4096 + 1024 * i, 1024).bitcast(BF16).rearrange("p (t d) -> p t d", t=T)
                    for i in range(3)]
        x1T = part(area, 7168, KD, S)
        xeT = [part(area, 7168 + 1024 * i, KD, P) for i in range(PAIRS)]
        h2_rest = part(area, 9216, D)
        squares2 = part(area, 10240, 512).bitcast(BF16)
        actT = part(area, 9216, KD, P)
        y_sb = part(area, 10240, 2, GROUP)
        gatherT = part(area, 13376, S)
        pick = [part(area, 13632 + 128 * i, 128).bitcast(BF16).rearrange("p (t s) -> p t s", t=T)
                for i in range(PAIRS)]
        pick_gated = [part(area, 13888 + 256 * i, T, P) for i in range(PAIRS)]
        bias_pick = [part(area, 14400 + 64 * i, 64).bitcast(BF16) for i in range(PAIRS)]
        onehot = part(area, 14528, T * TOPK, NE)
        gated_hot = part(area, 14784, T * TOPK, NE)
        route_tmp = part(area, 15040, T, NE)

        bank = [ctx.enter_context(nc.psum_tensor(f"bank{i}", [P, 512], F32)) for i in range(8)]

        g1_in, g1_turned, g1_ready = map(sem, ("g1_in", "g1_turned", "g1_ready"))
        x_in0, params_in, small_in, rel_in, bias_in = map(sem, ("x_in0", "params_in", "small_in", "rel_in", "bias_in"))
        x_in = [x_in0, sem("x_in1")]
        out_stored = sem("out_stored")
        w_first_full = [sem(f"w_first_full{i}") for i in range(4)]
        w_in_full = [None] + [sem(f"w_in_full{g}") for g in range(1, 6)]
        w_out_full = [sem(f"w_out_full{b}") for b in range(2)]
        extra_full = [sem(f"extra_full{i}") for i in range(EXTRA)]
        ring_full = [sem(f"ring_full{s}") for s in range(RING)]
        result_ready = sem("result_ready")
        pool_step, ident_ready, consts_ready, bias_split = map(sem, ("pool_step", "ident_ready", "consts_ready", "bias_split"))
        vec_step = sem("vec_step")
        sq1, root1, rstd1 = map(sem, ("sq1", "root1", "rstd1"))
        router_scaled, low_rank_ready = map(sem, ("router_scaled", "low_rank_ready"))
        params_turned, gains_ready = map(sem, ("params_turned", "gains_ready"))
        hT_psum, hT_written, hT_high_ready, hT_low_ready = map(
            sem, ("hT_psum", "hT_written", "hT_high_ready", "hT_low_ready"))
        w_high_ready, w_low_ready, units_used = map(sem, ("w_high_ready", "w_low_ready", "units_used"))
        proj_ready = sem("proj_ready")
        lr_psum, lrT_psum, lr_ready, z_psum, abs_z, log_ready = map(sem, ("lr_psum", "lrT_psum", "lr_ready", "z_psum", "abs_z", "log_ready"))
        qk_squared, qk_summed, qk_root, qk_normed = map(sem, ("qk_squared", "qk_summed", "qk_root", "qk_normed"))
        qkT_psum, qkT_ready = map(sem, ("qkT_psum", "qkT_ready"))
        score_psum, score_ready, max_ready, exp_ready, prob_ready = map(
            sem, ("score_psum", "score_ready", "max_ready", "exp_ready", "prob_ready"))
        glaq_psum, glaq_ready = map(sem, ("glaq_psum", "glaq_ready"))
        rev_psum, rev_exp, kdec_ready = map(sem, ("rev_psum", "rev_exp", "kdec_ready"))
        probT_psum, probT_ready = map(sem, ("probT_psum", "probT_ready"))
        u_psum, state_ready = map(sem, ("u_psum", "state_ready"))
        att_psum, att_ready = map(sem, ("att_psum", "att_ready"))
        gate_sig, gla_psum, gla_squared, gla_summed, gla_root, gla_normed = map(
            sem, ("gate_sig", "gla_psum", "gla_squared", "gla_summed", "gla_root", "gla_normed"))
        glaT_psum, glaT_ready = map(sem, ("glaT_psum", "glaT_ready"))
        att_mixed, mix_psum, x1_ready = map(sem, ("att_mixed", "mix_psum", "x1_ready"))
        sq2, root2, rstd2 = map(sem, ("sq2", "root2", "rstd2"))
        part0_ready, rest_ready, part1_ready, h2_ready = map(
            sem, ("part0_ready", "rest_ready", "part1_ready", "h2_ready"))
        x1T_psum, x1T_act, x1T_dve, logit_psum, top_ready, top_expd = map(
            sem, ("x1T_psum", "x1T_act", "x1T_dve", "logit_psum", "top_ready", "top_expd"))
        mask_ready, rank_psum, slots_ready, flags_ready = map(
            sem, ("mask_ready", "rank_psum", "slots_ready", "flags_ready"))
        gated_ready, bias_pick_ready = map(sem, ("gated_ready", "bias_pick_ready"))
        chunks_used, route_ready, pack_psum, pack_ready, hidden_psum = map(
            sem, ("chunks_used", "route_ready", "pack_psum", "pack_ready", "hidden_psum"))
        glu_clipped, lin_clipped, sig_ready, glu_ready, hidden_ready = map(
            sem, ("glu_clipped", "lin_clipped", "sig_ready", "glu_ready", "hidden_ready"))
        hiddenT_psum, hiddenT_ready, gatherT_psum, gatherT_ready = map(
            sem, ("hiddenT_psum", "hiddenT_ready", "gatherT_psum", "gatherT_ready"))
        y_psum, y_ready, comb_psum, comb_added = map(sem, ("y_psum", "y_ready", "comb_psum", "comb_added"))

        G1, G2, GN, GQ, GK = 0, KD, 2 * KD, 2 * KD + 1, 2 * KD + 2
        block = ctx.enter_context(nc.Block())

        def flag_column(quad, rnd):
            return (rnd - 1) * ITERS + quad

        def all_rounds(eng, run, no_more=None):
            run(0, 0, 0)
            with eng.Fori(1, ITERS) as it:
                run(it, it, 0)
            eng.wait_ge(flags_ready, 1)
            with eng.If(eng.value_load(flags[0:1, 24:25], min_val=0, max_val=1) != 0):
                done = eng.alloc_register("iterations_done")
                eng.reg_mov(done, ITERS)
                for rnd in range(1, ROUNDS):
                    with eng.Fori(0, ITERS) as quad:
                        col = eng.snap(quad + (rnd - 1) * ITERS)
                        flag = eng.value_load(flags[0:1, bass.ds(col, 1)], min_val=0, max_val=1)
                        with eng.If(flag != 0):
                            it = eng.snap(done, min_val=ITERS, max_val=ITERS * ROUNDS)
                            run(it, quad, rnd)
                            eng.reg_add(done, done, 1)
                        with eng.Else():
                            eng.nop()
                        eng.nop()
            with eng.Else():
                if no_more:
                    no_more()
                eng.nop()
            eng.nop()

        @block.sync
        def _(sp):
            for t in range(T):
                sp.dma_start(acc[:, t, :], x[0, t * P:(t + 1) * P, :]).then_inc(x_in[t], 16)

            def load_group(g):
                c = GROUP_COL[g]
                sp.dma_start(w_buf[g], w_in[0, :, c:c + GROUP].rearrange("(k p) n -> p k n", p=P))\
                    .then_inc(w_in_full[g], 16)

            def fill(buf, full, quad, c):
                job, r = divmod(c, JOB_CHUNKS)
                if r < 2 * KD:
                    k, e = divmod(r, 2)
                    src = moe_w_in[0, bass.ds(quad * EPI + 2 * job + e, 1), k * P:(k + 1) * P, :]
                    dst = buf.rearrange("p (a f) -> p a f", a=1)
                    src = src.rearrange("a p f -> p a f")
                else:
                    k = r - 2 * KD
                    src = moe_w_out[0, bass.ds(quad * EPI + 2 * job, 2), k * P:(k + 1) * P, :]
                    src = src.rearrange("a p d -> p a d")
                    dst = buf.rearrange("p (a d) -> p a d", a=2)
                sp.dma_start(dst, src).then_inc(full, 16)

            def fill_ring(slot, quad, c):
                fill(ring[:, slot, :], ring_full[slot], quad, c)

            def fill_extra(i):
                fill(extra[i], extra_full[i], 0, FIRST_EXTRA + i)

            for i in range(4):
                c = GROUP_COL[0]
                sp.dma_start(w_buf[0][:, 2 * i:2 * i + 2, :],
                             w_in[0, 2 * i * P:2 * (i + 1) * P, c:c + GROUP].rearrange("(k p) n -> p k n", p=P))\
                    .then_inc(w_first_full[i], 16)
            load_group(AK)
            sp.dma_start(params[8:16, :], norm2_g[0].rearrange("(k p) -> k p", p=P)).then_inc(params_in, 16)
            sp.dma_start(params[16:17, :], gla_norm_g).then_inc(params_in, 16)
            for row, g in ((17, q_norm_g), (18, k_norm_g)):
                for b in range(2):
                    sp.dma_start(params[row:row + 1, b * 64:b * 64 + 64], g).then_inc(params_in, 16)
            sp.dma_start(w_lr[:, :, :], w_in[0, :, LR_COL:LR_COL + GRANK].rearrange("(k p) n -> p k n", p=P))\
                .then_inc(small_in, 16)
            sp.dma_start(area[0:GRANK, o + 6528:o + 6784], gla_gate_up[0]).then_inc(small_in, 16)
            sp.dma_start(area[GRANK:GRANK + 1, o + 6528:o + 6784], gla_gate_bias).then_inc(small_in, 16)
            sp.dma_start(w_router[:, :, :], router_w[0].rearrange("(k p) n -> p k n", p=P)).then_inc(small_in, 16)
            sp.dma_start(b_router[:, :], bass.AP(router_b.tensor, router_b.offset, [[0, P], [1, NE]]))\
                .then_inc(small_in, 16)
            for t in range(T):
                keys = P * (t + 1)
                off = REL_CLIP + P * t - (keys - 1)
                sp.dma_start(rel[t], bass.AP(rel_bias.tensor, rel_bias.offset + off,
                                              [[1, P], [2 * REL_CLIP + 1, AH], [1, keys]])).then_inc(rel_in, 16)
            for i in range(3):
                rows = slice(32 * i, 32 * i + 32)
                sp.dma_start(b_in_raw[rows, :], moe_b_in[0]).then_inc(bias_in, 16)
                sp.dma_start(b_out_raw[rows, :], moe_b_out[0]).then_inc(bias_in, 16)

            def load_w_out(b):
                sp.dma_start(w_out_sb[:, 4 * b:4 * b + 4, :],
                             w_out[0, b * 512:(b + 1) * 512, :].rearrange("(k p) n -> p k n", p=P))\
                    .then_inc(w_out_full[b], 16)

            for g in (AV, GQK, GV, OG):
                sp.wait_ge(w_low_ready, UNITS * (g - 1))
                load_group(g)
            sp.wait_ge(bias_split, 1)
            fill_ring(5, 0, 5)
            for b in range(2):
                sp.wait_ge(w_low_ready, UNITS * (GV + b + 1))
                load_w_out(b)
            sp.wait_ge(units_used, UNITS * 6)
            for slot in range(5):
                fill_ring(slot, 0, slot)
            sp.wait_ge(gla_summed, 2)
            sp.wait_ge(att_psum, 2)
            for slot in range(6, 12):
                fill_ring(slot, 0, slot)
            fill_extra(0)
            sp.wait_ge(glaT_psum, 2)
            fill_extra(2)
            sp.wait_ge(att_mixed, 1)
            for slot in range(14, RING):
                fill_ring(slot, 0, slot + RING)
            sp.wait_ge(mix_psum, 4)
            fill_extra(1)
            for slot in range(12, 14):
                fill_ring(slot, 0, slot + RING)
            sp.wait_ge(h2_ready, 2)
            fill_extra(3)

            def run(it, quad, rnd):
                first = isinstance(it, int)
                for c in range(RING if first else 0, ITER_CHUNKS):
                    if first and FIRST_EXTRA + RING <= c < 2 * RING:
                        continue
                    sp.wait_ge(chunks_used, it * ITER_CHUNKS + c - RING + 1)
                    fill_ring(c % RING, quad, c)

            def store(n):
                dh, t = divmod(n, 2)
                cols = slice(dh * GROUP, (dh + 1) * GROUP)
                sp.dma_start(out[0, t * P:(t + 1) * P, cols], acc[:, t, cols]).then_inc(out_stored, 16)

            def store_after_round_0():
                for n in range(4):
                    sp.wait_ge(comb_added, 4 * PAIRS * ITERS - 3 + n)
                    store(n)

            all_rounds(sp, run, store_after_round_0)
            sp.wait_ge(result_ready, 1)
            with sp.If(sp.value_load(flags[0:1, 24:25], min_val=0, max_val=1) != 0):
                for n in range(4):
                    store(n)
            with sp.Else():
                sp.nop()
            sp.wait_ge(out_stored, 16 * 4)

        @block.gpsimd
        def _(pool):
            steps = [0]

            def step(ins):
                steps[0] += 1
                ins.then_inc(pool_step, 1)
                pool.wait_ge(pool_step, steps[0])

            step(pool.memset(ident[:, :], 0.0))
            step(pool.memset(eps[:, :], EPS))
            pool.affine_select(out=ident[:, :], in_=ident[:, :], compare_op=ALU.not_equal, fill=1.0,
                               base=0, pattern=[[-1, P]], channel_multiplier=1).then_inc(ident_ready, 1)
            pool.wait_ge(ident_ready, 1)
            step(pool.memset(ones[:, :], 1.0))
            step(pool.memset(lrT[0:32, :], 1.0))
            step(pool.memset(chunk_of[:, :], 0.0))
            step(pool.memset(state[:, :, :, :], 0.0))
            step(pool.memset(chunk_of[0:64, 0:1], 1.0))
            step(pool.memset(chunk_of[64:128, 1:2], 1.0))
            step(pool.affine_select(out=later[:, :], in_=ones[:, :], compare_op=ALU.is_gt, fill=0.0,
                                    base=0, pattern=[[-1, P]], channel_multiplier=1))
            step(pool.affine_select(out=before[:, :], in_=ones[:, :], compare_op=ALU.is_gt, fill=0.0,
                                    base=0, pattern=[[1, P]], channel_multiplier=-1))
            step(pool.memset(later[64:128, 0:64], 0.0))
            step(pool.iota(slot_iota[:, :], [[1, SLOTS]], base=0, channel_multiplier=0,
                           allow_small_or_imprecise_dtypes=True))
            step(pool.iota(expert_iota[:, :], [[1, NE]], base=0, channel_multiplier=0,
                           allow_small_or_imprecise_dtypes=True))
            step(pool.iota(pair_first[:, :], [[2, NE // 2]], base=0, channel_multiplier=0,
                           allow_small_or_imprecise_dtypes=True))
            for i in range(3):
                step(pool.iota(expert_diff[32 * i:32 * i + 32, :], [[-1, 2], [0, 64]], base=0,
                               channel_multiplier=1, allow_small_or_imprecise_dtypes=True))
            step(pool.memset(expert_diff[96:128, :], -5.0))
            pool.memset(bias_parts[96:128, :], 0.0).then_inc(consts_ready, 1)
            pool.wait_ge(bias_in, 96)
            for n in range(3):
                parts_of = bias_parts[:, n * D:(n + 1) * D]
                raw = b_in_raw[:, n * D:(n + 1) * D] if n < 2 else b_out_raw
                step(pool.tensor_copy(parts_of[0:96, :], raw[0:96, :]))
                step(pool.tensor_tensor(bias_rest[0:96, :], raw[0:96, :], parts_of[0:96, :], ALU.subtract))
                step(pool.tensor_copy(parts_of[0:64, :], bias_rest[0:64, :]))
                ins = pool.tensor_tensor(parts_of[0:32, :], bias_rest[0:32, :], parts_of[0:32, :], ALU.subtract)
                if n < 2:
                    step(ins)
            ins.then_inc(bias_split, 1)

        @block.scalar
        def _(act):
            act.dma_start(params[0:8, :], norm1_g[0].rearrange("(k p) -> k p", p=P)).then_inc(g1_in, 16)
            units = [0]

            def high_parts(count):
                for n in range(units[0], units[0] + count):
                    g, i = divmod(n, UNITS)
                    act.wait_ge(w_in_full[g] if g else w_first_full[i], 16)
                    if n >= SPLITS:
                        act.wait_ge(units_used, n - SPLITS + 1)
                    act.activation(w_high[n % SPLITS], w_buf[g][:, 2 * i:2 * i + 2, :], ACT.Copy)\
                        .then_inc(w_high_ready, 1)
                units[0] += count

            def hT_high_part(n):
                half, t = divmod(n, 2)
                act.wait_ge(hT_written, n + 1)
                act.activation(hT_high[:, 4 * half:4 * half + 4, t * P:(t + 1) * P],
                               hT[:, 4 * half:4 * half + 4, t * P:(t + 1) * P], ACT.Copy)\
                    .then_inc(hT_high_ready, 1)

            hT_high_part(0)
            hT_high_part(1)
            high_parts(1)
            hT_high_part(2)
            hT_high_part(3)
            high_parts(1)
            act.wait_ge(ident_ready, 1)
            for t in range(T):
                act.wait_ge(x_in[t], 16)
                act.activation(x_squares[:, t, :], acc[:, t, :], ACT.Square, accum_out=stat[:, t:t + 1])\
                    .then_inc(sq1, 1)
                if t == 0:
                    high_parts(1)
            act.wait_ge(sq1, 2)
            act.activation(stat[:, 2:4], stat[:, 0:2], ACT.Sqrt, bias=eps[:, 0:1], scale=1.0 / D).then_inc(root1, 1)
            high_parts(4)
            act.wait_ge(rstd1, 1)

            def project_out(g):
                act.wait_ge(units_used, UNITS * (g + 1))
                for t in range(T):
                    act.activation(proj[:, t, g * GROUP:(g + 1) * GROUP], bank[4 + 2 * (g % 2) + t][:, :],
                                   ACT.Copy, scale=stat[:, t:t + 1]).then_inc(proj_ready, 1)

            def squares(g):
                act.wait_ge(proj_ready, 2 * g + 2)
                if g:
                    act.wait_ge(qk_summed, 2 * g)
                for t in range(T):
                    act.activation(square[:, t * GROUP:(t + 1) * GROUP], proj[:, t, g * GROUP:(g + 1) * GROUP],
                                   ACT.Square).then_inc(qk_squared, 1)
                act.wait_ge(qk_summed, 2 * g + 2)
                act.activation(stat[:, 32 + 16 * g:48 + 16 * g], stat[:, 64 + 16 * g:80 + 16 * g], ACT.Sqrt,
                               bias=eps[:, 0:1], scale=1.0 / ADH).then_inc(qk_root, 1)

            project_out(AQ)
            squares(0)
            high_parts(4)
            project_out(AK)
            squares(1)
            act.wait_ge(lr_psum, 1)
            for t in range(T):
                act.activation(low_rank[:, t, :], bank[0][:, t * GRANK:(t + 1) * GRANK], ACT.Copy,
                               scale=stat[:, t:t + 1]).then_inc(low_rank_ready, 1)
            high_parts(2)
            act.wait_ge(lrT_psum, 1)
            act.wait_ge(consts_ready, 1)
            act.activation(lrT[0:GRANK, :], bank[1][0:GRANK, 0:S], ACT.Copy).then_inc(lr_ready, 1)
            high_parts(2)
            project_out(AV)
            for n in range(4):
                act.wait_ge(qkT_psum, n + 1)
                dst = (att_qT, att_kT)[n // 2]
                gain = (GQ, GK)[n // 2]
                act.activation(dst[:, 2 * (n % 2):2 * (n % 2) + 2, :],
                               bank[n][:, :].rearrange("p (a b) -> p a b", a=2), ACT.Copy,
                               scale=gains[:, gain:gain + 1]).then_inc(qkT_ready, 1)
            high_parts(4)
            project_out(GQK)
            act.wait_ge(glaq_psum, 1)
            act.activation(gla_qT, bank[3][:, :].rearrange("p (a b) -> p a b", a=2), ACT.Copy,
                           scale=GDK ** -0.5).then_inc(glaq_ready, 1)

            def exps(t):
                act.wait_ge(max_ready, t + 1)
                for h in range(AH):
                    ins = act.activation(scores[t][:, h, :], scores[t][:, h, :], ACT.Exp,
                                         bias=stat[:, 8 + 8 * t + h:9 + 8 * t + h],
                                         accum_out=stat[:, 96 + 8 * t + h:97 + 8 * t + h])
                ins.then_inc(exp_ready, 1)

            act.wait_ge(z_psum, 1)
            z = bank[2][:, :].rearrange("p (t n) -> p t n", t=T)
            act.activation(decay_tok, z, ACT.Abs).then_inc(abs_z, 1)
            act.wait_ge(abs_z, 1)
            act.activation(k_dec, decay_tok, ACT.Exp, scale=-1.0).then_inc(abs_z, 1)
            act.wait_ge(abs_z, 2)
            act.wait_ge(consts_ready, 1)
            act.activation(decay_tok, k_dec, ACT.Ln, bias=ones[:, 0:1]).then_inc(abs_z, 1)
            high_parts(2)
            exps(0)
            high_parts(2)
            project_out(GV)
            act.wait_ge(rev_psum, 2)
            act.activation(decay_tok, bank[4][:, :].rearrange("p (t n) -> p t n", t=T), ACT.Exp,
                           scale=1.0 / GTAU).then_inc(rev_exp, 1)
            act.activation(stat[:, 24:32], bank[5][:, 0:8], ACT.Exp, scale=1.0 / GTAU).then_inc(rev_exp, 1)
            high_parts(1)
            exps(1)
            project_out(OG)
            for n in range(2):
                act.wait_ge(probT_psum, n + 1)
                act.activation(probT[0][:, 4 * n:4 * n + 4, 0:P],
                               bank[n][:, :].rearrange("p (a b) -> p a b", a=4), ACT.Copy).then_inc(probT_ready, 1)
            act.wait_ge(proj_ready, 12)
            act.wait_ge(bias_split, 1)
            act.activation(out_gate, proj[:, :, 5 * GROUP:6 * GROUP], ACT.Sigmoid).then_inc(gate_sig, 1)
            for n in range(4):
                act.wait_ge(probT_psum, n + 3)
                dst = probT[0][:, 4 * n:4 * n + 4, P:S] if n < 2 else probT[1][:, 4 * (n - 2):4 * (n - 2) + 4, :]
                act.activation(dst, bank[(0, 1, 6, 7)[n]][:, :].rearrange("p (a b) -> p a b", a=4), ACT.Copy)\
                    .then_inc(probT_ready, 1)
            for n in range(2):
                act.wait_ge(att_psum, n + 1)
                act.activation(mixT[:, 4 + 2 * n:6 + 2 * n, :], bank[n][:, :].rearrange("p (a b) -> p a b", a=2),
                               ACT.Copy).then_inc(att_ready, 1)
            for t in range(T):
                act.wait_ge(gla_psum, t + 1)
                act.activation(square[:, t * GROUP:(t + 1) * GROUP], bank[2 + t][:, :], ACT.Square)\
                    .then_inc(gla_squared, 1)
            act.wait_ge(gla_summed, 2)
            act.activation(stat[:, 120:128], stat[:, 112:120], ACT.Sqrt, bias=eps[:, 0:1], scale=1.0 / GDV)\
                .then_inc(gla_root, 1)
            for n in range(2):
                act.wait_ge(glaT_psum, n + 1)
                act.activation(mixT[:, 2 * n:2 * n + 2, :], bank[4 + n][:, :].rearrange("p (a b) -> p a b", a=2),
                               ACT.Copy, scale=gains[:, GN:GN + 1]).then_inc(glaT_ready, 1)
            for t in range(T):
                act.wait_ge(x1_ready, (2, 4)[t])
                act.activation(squares2, acc[:, t, :], ACT.Square, accum_out=stat[:, t:t + 1]).then_inc(sq2, 1)
                act.wait_ge(sq2, t + 1)
                act.activation(stat[:, 2 + t:3 + t], stat[:, t:t + 1], ACT.Sqrt, bias=eps[:, 0:1], scale=1.0 / D)\
                    .then_inc(root2, 1)
                act.wait_ge(x1T_psum, 2 * t + 1)
                act.activation(x1T[:, 0:4, t * P:(t + 1) * P], bank[2 + 2 * t][:, :].rearrange("p (a b) -> p a b", a=4),
                               ACT.Copy).then_inc(x1T_act, 1)
                act.wait_ge(rstd2, t + 1)
                act.activation(h2_parts[0][:, t, :], acc[:, t, :], ACT.Copy, scale=stat[:, t:t + 1])\
                    .then_inc(part0_ready, 1)
                act.wait_ge(rest_ready, t + 1)
                act.activation(h2_parts[1][:, t, :], h2_rest, ACT.Copy).then_inc(part1_ready, 1)
            for t in range(T):
                act.wait_ge(top_ready, t + 1)
                act.activation(top_exp[:, t, :], top_val[:, t, 0:TOPK], ACT.Exp, bias=stat[:, 4 + t:5 + t])\
                    .then_inc(top_expd, 1)

            def run(it, quad, rnd):
                for a in range(PAIRS):
                    j = it * PAIRS + a
                    for hf in range(2):
                        act.wait_ge(glu_clipped, 2 * j + hf + 1)
                        act.activation(sig[:, hf, :], glu_c[:, hf, :], ACT.Sigmoid, scale=ALPHA)\
                            .then_inc(sig_ready, 1)
                    for hf in range(2):
                        act.wait_ge(hiddenT_psum, 2 * j + hf + 1)
                        act.activation(actT[:, 4 * hf:4 * hf + 4, :],
                                       bank[4 + hf][:, :].rearrange("p (a b) -> p a b", a=4), ACT.Copy)\
                            .then_inc(hiddenT_ready, 1)
                    act.wait_ge(gatherT_psum, j + 1)
                    act.activation(gatherT, bank[0][:, 0:S], ACT.Copy).then_inc(gatherT_ready, 1)
                    for dh in range(2):
                        act.wait_ge(y_psum, 2 * j + dh + 1)
                        act.activation(y_sb[:, dh, :], bank[6 + dh][:, :], ACT.Copy).then_inc(y_ready, 1)

            all_rounds(act, run)

        @block.vector
        def _(dve):
            steps = [0]

            def step(ins):
                steps[0] += 1
                ins.then_inc(vec_step, 1)
                dve.wait_ge(vec_step, steps[0])

            dve.wait_ge(g1_turned, 1)
            dve.tensor_copy(gains[:, 0:KD], bank[6][:, 0:KD]).then_inc(g1_ready, 1)
            dve.wait_ge(g1_ready, 1)
            units = [0]

            def low_parts(count):
                for n in range(units[0], units[0] + count):
                    g, i = divmod(n, UNITS)
                    dve.wait_ge(w_high_ready, n + 1)
                    dve.tensor_tensor(w_low[n % SPLITS], w_buf[g][:, 2 * i:2 * i + 2, :], w_high[n % SPLITS],
                                      ALU.subtract)\
                        .then_inc(w_low_ready, 1)
                units[0] += count

            def hT_quarter(n):
                half, t = divmod(n, 2)
                dve.wait_ge(hT_psum, n + 1)
                g = gains[:, G1 + 4 * half:G1 + 4 * half + 4].unsqueeze(2)
                dve.tensor_tensor(hT[:, 4 * half:4 * half + 4, t * P:(t + 1) * P],
                                  bank[2 * t + half][:, :].rearrange("p (c s) -> p c s", c=4),
                                  g.to_broadcast([P, 4, P]), ALU.mult).then_inc(hT_written, 1)

            def hT_low_part(n):
                half, t = divmod(n, 2)
                dve.wait_ge(hT_high_ready, n + 1)
                at = slice(4 * half, 4 * half + 4), slice(t * P, (t + 1) * P)
                dve.tensor_tensor(hT_low[:, at[0], at[1]], hT[:, at[0], at[1]], hT_high[:, at[0], at[1]],
                                  ALU.subtract).then_inc(hT_low_ready, 1)

            hT_quarter(0)
            hT_quarter(1)
            hT_low_part(0)
            hT_low_part(1)
            hT_quarter(2)
            hT_quarter(3)
            low_parts(1)
            hT_low_part(2)
            hT_low_part(3)
            low_parts(2)
            dve.wait_ge(root1, 1)
            dve.reciprocal(stat[:, 0:2], stat[:, 2:4]).then_inc(rstd1, 1)
            low_parts(2)
            dve.wait_ge(params_turned, 1)
            dve.tensor_copy(gains[:, KD:], bank[7][:, KD:19]).then_inc(gains_ready, 1)
            low_parts(2)

            def normalise(g):
                for t in range(T):
                    dve.wait_ge(qk_squared, 2 * g + t + 1)
                    dve.tensor_reduce(stat[:, 64 + 16 * g + 8 * t:72 + 16 * g + 8 * t],
                                      square[:, t * GROUP:(t + 1) * GROUP].rearrange("p (h d) -> p h d", h=AH),
                                      AX, ALU.add).then_inc(qk_summed, 1)
                dve.wait_ge(qk_root, g + 1)
                r = stat[:, 32 + 16 * g:48 + 16 * g]
                step(dve.reciprocal(r, r))
                for t in range(T):
                    v = proj[:, t, g * GROUP:(g + 1) * GROUP].rearrange("p (h d) -> p h d", h=AH)
                    rs = stat[:, 32 + 16 * g + 8 * t:40 + 16 * g + 8 * t].unsqueeze(2)
                    dve.tensor_tensor(v, v, rs.to_broadcast([P, AH, ADH]), ALU.mult).then_inc(qk_normed, 1)

            normalise(0)
            low_parts(4)
            normalise(1)
            low_parts(4)
            dve.wait_ge(small_in, 80)
            dve.wait_ge(gains_ready, 1)
            dve.tensor_tensor(w_router[:, :, :], w_router[:, :, :],
                              gains[:, G2:G2 + KD].unsqueeze(2).to_broadcast([P, KD, NE]), ALU.mult)\
                .then_inc(router_scaled, 1)
            low_parts(4)
            dve.wait_ge(rel_in, 32)
            for t in range(T):
                step(dve.memset(rel[t][0:CHUNK, :, 0:CHUNK], MASK_VALUE))

            def add_bias(t):
                if t == 0:
                    for b in range(2):
                        dve.wait_ge(score_psum, b + 1)
                        dve.scalar_tensor_tensor(scores[0][:, b::2, :], bank[b][:, :].rearrange("p (a k) -> p a k", a=4),
                                                 ADH ** -0.5, rel[0][:, b::2, ::-1], ALU.mult, ALU.add)\
                            .then_inc(score_ready, 1)
                else:
                    for n in range(4):
                        b, half = n % 2, n // 2
                        dve.wait_ge(score_psum, 3 + n)
                        dve.scalar_tensor_tensor(scores[1][:, 4 * half + b:4 * half + b + 3:2, :],
                                                 bank[n][:, :].rearrange("p (a k) -> p a k", a=2),
                                                 ADH ** -0.5, rel[1][:, 4 * half + b:4 * half + b + 3:2, ::-1],
                                                 ALU.mult, ALU.add).then_inc(score_ready, 1)
                dve.wait_ge(score_ready, (2, 6)[t])
                m = stat[:, 8 + 8 * t:16 + 8 * t]
                step(dve.tensor_reduce(m, scores[t], AX, ALU.max))
                dve.tensor_scalar(m, m, -1.0, None, ALU.mult).then_inc(max_ready, 1)

            def scale_probs(t):
                dve.wait_ge(exp_ready, t + 1)
                r = stat[:, 96 + 8 * t:104 + 8 * t]
                step(dve.reciprocal(r, r))
                dve.tensor_tensor(scores[t], scores[t], r.unsqueeze(2).to_broadcast([P, AH, P * (t + 1)]), ALU.mult)\
                    .then_inc(prob_ready, 1)

            add_bias(0)
            low_parts(1)
            dve.wait_ge(abs_z, 3)
            dve.scalar_tensor_tensor(log_a, bank[2][:, :].rearrange("p (t n) -> p t n", t=T), 0.0, decay_tok,
                                     ALU.min, ALU.subtract).then_inc(log_ready, 1)
            low_parts(1)
            scale_probs(0)
            low_parts(2)
            add_bias(1)
            low_parts(1)
            dve.wait_ge(rev_exp, 1)
            dve.tensor_tensor(k_dec, proj[:, :, GQK * GROUP + 256:GQK * GROUP + 512], decay_tok, ALU.mult)\
                .then_inc(kdec_ready, 1)
            scale_probs(1)
            dve.wait_ge(u_psum, 4)
            dve.wait_ge(rev_exp, 2)
            for n in range(NCH):
                t, c = divmod(n, 2)
                ub = bank[2 + 2 * c + t]
                for pr in range(2):
                    for b in range(2):
                        rows, cols = slice(64 * b, 64 * b + 64), slice(P * b, P * b + P)
                        u = ub[rows, pr * S + P * b:pr * S + P * b + P]
                        if n == 0:
                            ins = dve.tensor_copy(state[rows, n, pr, cols], u)
                        else:
                            ins = dve.scalar_tensor_tensor(state[rows, n, pr, cols], state[rows, n - 1, pr, cols],
                                                           stat[rows, 24 + 4 * pr + n:25 + 4 * pr + n], u,
                                                           ALU.mult, ALU.add)
                ins.then_inc(state_ready, 1)
                dve.wait_ge(state_ready, n + 1)
            dve.wait_ge(gate_sig, 1)
            step(dve.tensor_tensor(out_gate, out_gate, proj[:, :, 5 * GROUP:6 * GROUP], ALU.mult))
            for t in range(T):
                dve.wait_ge(gla_squared, t + 1)
                dve.tensor_reduce(stat[:, 112 + 4 * t:116 + 4 * t],
                                  square[:, t * GROUP:(t + 1) * GROUP].rearrange("p (h d) -> p h d", h=GH),
                                  AX, ALU.add).then_inc(gla_summed, 1)
            dve.wait_ge(gla_root, 1)
            step(dve.reciprocal(stat[:, 120:128], stat[:, 120:128]))
            for t in range(T):
                for h in range(GH):
                    cols = slice(h * GDV, (h + 1) * GDV)
                    ins = dve.scalar_tensor_tensor(gla_o[:, t, cols], bank[2 + t][:, cols],
                                                   stat[:, 120 + 4 * t + h:121 + 4 * t + h],
                                                   out_gate[:, t, cols], ALU.mult, ALU.mult)
                ins.then_inc(gla_normed, 1)

            def residual(t, dh):
                dve.wait_ge(mix_psum, 2 * t + dh + 1)
                v = acc[:, t, dh * GROUP:(dh + 1) * GROUP]
                dve.tensor_tensor(v, bank[(6, 7, 0, 1)[2 * t + dh]][:, :], v, ALU.add).then_inc(x1_ready, 1)

            def x1_turned(t):
                dve.wait_ge(x1T_psum, 2 * t + 2)
                dve.tensor_copy(x1T[:, 4:8, t * P:(t + 1) * P], bank[3 + 2 * t][:, :].rearrange("p (a b) -> p a b", a=4))\
                    .then_inc(x1T_dve, 1)

            def rms(t):
                dve.wait_ge(root2, t + 1)
                dve.reciprocal(stat[:, t:t + 1], stat[:, 2 + t:3 + t]).then_inc(rstd2, 1)

            def split_rest(t):
                dve.wait_ge(part0_ready, t + 1)
                dve.scalar_tensor_tensor(h2_rest, acc[:, t, :], stat[:, t:t + 1], h2_parts[0][:, t, :],
                                         ALU.mult, ALU.subtract).then_inc(rest_ready, 1)

            def split_last(t):
                dve.wait_ge(part1_ready, t + 1)
                dve.tensor_tensor(h2_parts[2][:, t, :], h2_rest, h2_parts[1][:, t, :], ALU.subtract)\
                    .then_inc(h2_ready, 1)

            def choose(t):
                dve.wait_ge(logit_psum, t + 1)
                logit = route_tmp[:, t, :]
                step(dve.scalar_tensor_tensor(logit, bank[6 + t][:, 0:NE], stat[:, t:t + 1], b_router[:, :],
                                              ALU.mult, ALU.add))
                step(dve.max(top_val[:, t, :], logit))
                step(dve.max_index(top_idx[:, t, :], top_val[:, t, :], logit))
                dve.tensor_scalar(stat[:, 4 + t:5 + t], top_val[:, t, 0:1], -1.0, None, ALU.mult).then_inc(top_ready, 1)
                step(dve.tensor_copy(top_idx_f[:, t, :], top_idx[:, t, :]))
                step(dve.tensor_tensor(onehot[:, TOPK * t:TOPK * (t + 1), :],
                                       expert_iota[:, :].unsqueeze(1).to_broadcast([P, TOPK, NE]),
                                       top_idx_f[:, t, 0:TOPK].unsqueeze(2).to_broadcast([P, TOPK, NE]),
                                       ALU.is_equal))
                dve.tensor_reduce(mask[:, t, :], onehot[:, TOPK * t:TOPK * (t + 1), :].rearrange("p k e -> p e k"),
                                  AX, ALU.add).then_inc(mask_ready, 1)

            def pick_biases(a, quad):
                dve.tensor_scalar(bias_pick[a], expert_diff[:, :], pair_first[:, bass.ds(quad * PAIRS + a, 1)], None,
                                  ALU.is_equal).then_inc(bias_pick_ready, 1)

            residual(0, 0)
            residual(0, 1)
            residual(1, 0)
            x1_turned(0)
            rms(0)
            split_rest(0)
            residual(1, 1)
            split_last(0)
            x1_turned(1)
            rms(1)
            choose(0)
            split_rest(1)
            choose(1)
            pick_biases(0, 0)
            split_last(1)
            dve.wait_ge(rank_psum, 1)
            rank = route_tmp
            step(dve.scalar_tensor_tensor(rank, bank[4][:, 0:T * NE].rearrange("p (t e) -> p t e", t=T), 1.0,
                                          mask[:, :, :], ALU.add, ALU.mult))
            for r in range(ROUNDS):
                ins = dve.tensor_scalar(slot_of[:, :, r, :], rank, -1.0 - SLOTS * r, None, ALU.add)
            ins.then_inc(slots_ready, 1)
            dve.wait_ge(slots_ready, 1)

            def find_rounds():
                step(dve.tensor_reduce(counts[0:1, 32:40], bank[5][0:1, 0:NE].rearrange("p (q e) -> p q e", e=EPI),
                                       AX, ALU.max))
                for r in range(1, ROUNDS):
                    dve.tensor_scalar(flags[0:1, flag_column(0, r):flag_column(0, r) + ITERS], counts[0:1, 32:40],
                                      float(SLOTS * r), None, ALU.is_gt)
                step(dve.tensor_reduce(counts[0:1, 40:41], counts[0:1, 32:40], AX, ALU.max))
                dve.tensor_scalar(flags[0:1, 24:25], counts[0:1, 40:41], float(SLOTS), None, ALU.is_gt)\
                    .then_inc(flags_ready, 1)

            def spread_gates():
                dve.wait_ge(top_expd, 2)
                step(dve.tensor_reduce(stat[:, 4:6], top_exp[:, :, :], AX, ALU.add))
                step(dve.reciprocal(stat[:, 4:6], stat[:, 4:6]))
                step(dve.tensor_tensor(top_exp[:, :, :], top_exp[:, :, :],
                                       stat[:, 4:6].unsqueeze(2).to_broadcast([P, T, TOPK]), ALU.mult))
                for t in range(T):
                    ins = dve.tensor_tensor(gated_hot[:, TOPK * t:TOPK * (t + 1), :], onehot[:, TOPK * t:TOPK * (t + 1), :],
                                            top_exp[:, t, :].unsqueeze(2).to_broadcast([P, TOPK, NE]), ALU.mult)
                step(ins)
                for t in range(T):
                    ins = dve.tensor_reduce(gates[:, t, :], gated_hot[:, TOPK * t:TOPK * (t + 1), :].rearrange("p k e -> p e k"),
                                      AX, ALU.add)
                step(ins)

            def route(j, a, quad, rnd, gated):
                for e in range(2):
                    for t in range(T):
                        n = quad * EPI + 2 * a + e
                        at = slot_of[:, t, rnd, bass.ds(n, 1)]
                        if gated:
                            ins = dve.tensor_scalar(pick_gated[a][:, t, e * SLOTS:(e + 1) * SLOTS], slot_iota[:, :],
                                                    at, gates[:, t, bass.ds(n, 1)], ALU.is_equal, ALU.mult)
                        else:
                            ins = dve.tensor_scalar(pick[a][:, t, e * SLOTS:(e + 1) * SLOTS], slot_iota[:, :],
                                                    at, None, ALU.is_equal)
                ins.then_inc(gated_ready if gated else route_ready, 1)

            def packed(j, a, halves=(0, 1)):
                for n in halves:
                    dve.wait_ge(pack_psum, 2 * j + n + 1)
                    g = gains[:, G2 + 4 * n:G2 + 4 * n + 4].unsqueeze(2)
                    dve.tensor_tensor(xeT[a][:, 4 * n:4 * n + 4, :], bank[6 + n][:, :].rearrange("p (c s) -> p c s", c=4),
                                      g.to_broadcast([P, 4, P]), ALU.mult).then_inc(pack_ready, 1)

            def hidden(j):
                for hf in range(2):
                    dve.wait_ge(hidden_psum, 4 * j + 2 * hf + 1)
                    dve.tensor_scalar(glu_c[:, hf, :], bank[hf][:, :], LIMIT, None, ALU.min).then_inc(glu_clipped, 1)
                    dve.wait_ge(hidden_psum, 4 * j + 2 * hf + 2)
                    dve.tensor_scalar(lin_c[:, hf, :], bank[2 + hf][:, :], LIMIT, -LIMIT, ALU.min, ALU.max)\
                        .then_inc(lin_clipped, 1)
                for hf in range(2):
                    dve.wait_ge(sig_ready, 2 * j + hf + 1)
                    dve.tensor_tensor(sig[:, hf, :], glu_c[:, hf, :], sig[:, hf, :], ALU.mult).then_inc(glu_ready, 1)
                    dve.wait_ge(glu_ready, 2 * j + hf + 1)
                    dve.scalar_tensor_tensor(act_t[:, hf, :], lin_c[:, hf, :], 1.0, sig[:, hf, :], ALU.add, ALU.mult)\
                        .then_inc(hidden_ready, 1)

            def combine(j):
                for n in range(4):
                    dh, t = divmod(n, 2)
                    dve.wait_ge(comb_psum, 3 * j + max(n, 1))
                    v = acc[:, t, dh * GROUP:(dh + 1) * GROUP]
                    dve.tensor_tensor(v, bank[4 + n][:, :], v, ALU.add).then_inc(comb_added, 1)

            def run(it, quad, rnd):
                j = it * PAIRS
                first = isinstance(it, int)
                if not first:
                    dve.wait_ge(comb_psum, 3 * j)
                    pick_biases(0, quad)
                route(j, 0, quad, rnd, False)
                if first:
                    packed(0, 0, (0,))
                    spread_gates()
                    find_rounds()
                pick_biases(1, quad)
                route(j + 1, 1, quad, rnd, False)
                route(j, 0, quad, rnd, True)
                route(j + 1, 1, quad, rnd, True)
                packed(j, 0, (1,) if first else (0, 1))
                hidden(j)
                packed(j + 1, 1)
                combine(j)
                hidden(j + 1)
                combine(j + 1)

            all_rounds(dve, run)
            dve.drain().then_inc(result_ready, 1)

        @block.tensor
        def _(pe):
            pe.wait_ge(ident_ready, 1)
            pe.wait_ge(g1_in, 16)
            pe.transpose(bank[6][:, 0:KD], params[0:KD, :], ident[0:KD, 0:KD]).then_inc(g1_turned, 1)
            for half in range(2):
                for t in range(T):
                    pe.wait_ge(x_in[t], 16)
                    for k in range(4 * half, 4 * half + 4):
                        ins = pe.transpose(bank[2 * t + half][:, (k % 4) * P:(k % 4 + 1) * P],
                                           acc[:, t, k * P:(k + 1) * P], ident[:, :])
                    ins.then_inc(hT_psum, 1)

            def project(g, middle=None):
                if g >= 2:
                    pe.wait_ge(proj_ready, 2 * (g - 1))
                if g == 1:
                    pe.wait_ge(gains_ready, 1)
                for i in range(UNITS):
                    if i == 2 and middle:
                        middle()
                    n = g * UNITS + i
                    pe.wait_ge(w_low_ready, n + 1)
                    high, low = w_high[n % SPLITS], w_low[n % SPLITS]
                    for t in range(T):
                        if g == 0:
                            pe.wait_ge(hT_low_ready, 2 * (i // 2) + t + 1)
                        for kk in range(2):
                            k = 2 * i + kk
                            for h, w in ((hT_high, high), (hT_high, low), (hT_low, high)):
                                ins = pe.matmul(bank[4 + 2 * (g % 2) + t][:, :], h[:, k, t * P:(t + 1) * P], w[:, kk, :],
                                                start=(k == 0 and w is high and h is hT_high),
                                                stop=(k == KD - 1 and h is hT_low))
                    ins.then_inc(units_used, 1)

            project(AQ)
            pe.wait_ge(params_in, 16 * 6)
            pe.transpose(bank[7][:, 0:19], params[0:19, :], ident[0:19, 0:19]).then_inc(params_turned, 1)
            project(AK)
            pe.wait_ge(small_in, 80)
            for t in range(T):
                for k in range(KD):
                    ins = pe.matmul(bank[0][:, t * GRANK:(t + 1) * GRANK], hT[:, k, t * P:(t + 1) * P], w_lr[:, k, :],
                                    start=(k == 0), stop=(k == KD - 1))
            ins.then_inc(lr_psum, 1)

            def turn_low_rank():
                pe.wait_ge(low_rank_ready, 2)
                for t in range(T):
                    ins = pe.transpose(bank[1][0:GRANK, t * P:(t + 1) * P], low_rank[:, t, :], ident[:, :])
                ins.then_inc(lrT_psum, 1)

            project(AV, turn_low_rank)
            pe.wait_ge(lr_ready, 1)
            for g in range(2):
                pe.wait_ge(qk_normed, 2 * g + 2)
                for pr in range(4):
                    for t in range(T):
                        ins = pe.transpose(bank[2 * g + pr // 2][:, (pr % 2) * S + t * P:(pr % 2) * S + (t + 1) * P],
                                           proj[:, t, g * GROUP + pr * P:g * GROUP + (pr + 1) * P], ident[:, :])
                    if pr % 2:
                        ins.then_inc(qkT_psum, 1)
            project(GQK)

            def score(t):
                keys = P * (t + 1)
                if t == 0:
                    pe.wait_ge(qkT_ready, 4)
                else:
                    pe.wait_ge(score_ready, 2)
                    pe.wait_ge(log_ready, 1)
                    pe.wait_ge(glaq_ready, 1)
                for half in range(1 if t == 0 else 2):
                    width = 4 if t == 0 else 2
                    for i in range(width):
                        pr = half * width + i
                        for b in range(2):
                            rows = slice(64 * b, 64 * b + 64)
                            ins = pe.matmul(bank[2 * half + b][:, i * keys:(i + 1) * keys],
                                            att_qT[rows, pr, t * P:(t + 1) * P], att_kT[rows, pr, 0:keys],
                                            start=True, stop=True)
                            if i == width - 1:
                                ins.then_inc(score_psum, 1)

            score(0)
            for t in range(T):
                ins = pe.matmul(bank[2][:, t * S:(t + 1) * S], lrT[0:GRANK + 1, t * P:(t + 1) * P], gate_up,
                                start=True, stop=True)
            ins.then_inc(z_psum, 1)
            pe.wait_ge(proj_ready, 2 * GQK + 2)
            for pr in range(2):
                for t in range(T):
                    c = GQK * GROUP + pr * P
                    ins = pe.transpose(bank[3][:, pr * S + t * P:pr * S + (t + 1) * P], proj[:, t, c:c + P], ident[:, :])
            ins.then_inc(glaq_psum, 1)
            project(GV)
            score(1)
            pe.wait_ge(proj_ready, 10)
            for t in range(T):
                ins = pe.matmul(bank[4][:, t * S:(t + 1) * S], later[:, :], log_a[:, t, :], start=True, stop=True)
            ins.then_inc(rev_psum, 1)
            for pr in range(2):
                for t in range(T):
                    ins = pe.matmul(bank[5][:, 4 * pr + 2 * t:4 * pr + 2 * t + 2], log_a[:, t, pr * P:(pr + 1) * P],
                                    chunk_of[:, :], start=True, stop=True)
            ins.then_inc(rev_psum, 1)
            project(OG)
            pe.wait_ge(prob_ready, 1)
            pe.wait_ge(score_ready, 6)
            for h in range(AH):
                ins = pe.transpose(bank[h // 4][:, (h % 4) * P:(h % 4 + 1) * P], scores[0][:, h, :], ident[:, :])
                if h % 4 == 3:
                    ins.then_inc(probT_psum, 1)
            pe.wait_ge(kdec_ready, 1)
            pe.wait_ge(rev_exp, 2)
            for t in range(T):
                for pr in range(2):
                    for c in range(2):
                        rows = slice(64 * c, 64 * c + 64)
                        col = GV * GROUP + pr * S
                        ins = pe.matmul(bank[2 + 2 * c + t][:, pr * S:(pr + 1) * S], k_dec[rows, t, pr * P:(pr + 1) * P],
                                        proj[rows, t, col:col + S], start=True, stop=True)
                        if pr:
                            ins.then_inc(u_psum, 1)
            pe.wait_ge(prob_ready, 2)
            pe.wait_ge(probT_ready, 2)
            pe.wait_ge(proj_ready, 12)
            for kt in range(2):
                for h in range(AH):
                    ins = pe.transpose(bank[6 * kt + h // 4][:, (h % 4) * P:(h % 4 + 1) * P],
                                       scores[1][:, h, kt * P:(kt + 1) * P], ident[:, :])
                    if h % 4 == 3:
                        ins.then_inc(probT_psum, 1)
            pe.wait_ge(probT_ready, 6)
            for pr in range(4):
                for b in range(2):
                    h = 2 * pr + b
                    o_ = bank[pr // 2][64 * b:64 * b + 64, (pr % 2) * S:(pr % 2) * S + S]
                    vc = AV * GROUP + h * ADH
                    pe.matmul(o_, proj[:, 0, vc:vc + ADH], probT[0][:, h, :], start=True, stop=False)
                    ins = pe.matmul(o_[:, P:S], proj[:, 1, vc:vc + ADH], probT[1][:, h, :], start=False, stop=True)
                if pr % 2:
                    ins.then_inc(att_psum, 1)
            for n in range(NCH):
                t, c = divmod(n, 2)
                pe.wait_ge(state_ready, 4 if n == 0 else n + 1)
                for pr in range(2):
                    ins = pe.matmul(bank[2 + t][64 * c:64 * c + 64, pr * S:(pr + 1) * S],
                                    gla_qT[:, pr, n * CHUNK:(n + 1) * CHUNK], state[:, n, pr, :], start=True, stop=True)
                if c:
                    ins.then_inc(gla_psum, 1)

            def mix(t, first_k, cols=(0, 1)):
                for dh in cols:
                    for k in range(first_k, first_k + 4):
                        ins = pe.matmul(bank[(6, 7, 0, 1)[2 * t + dh]][:, :], mixT[:, k, t * P:(t + 1) * P],
                                        w_out_sb[:, k, dh * GROUP:(dh + 1) * GROUP], start=(k == 4), stop=(k == 3))
                    if first_k == 0:
                        ins.then_inc(mix_psum, 1)
                    elif t == 1 and dh == 1:
                        ins.then_inc(att_mixed, 1)

            def turn_x1(t, half):
                pe.wait_ge(x1_ready, 2 * t + half + 1)
                for k in range(4 * half, 4 * half + 4):
                    ins = pe.transpose(bank[2 + 2 * t + half][:, (k % 4) * P:(k % 4 + 1) * P],
                                       acc[:, t, k * P:(k + 1) * P], ident[:, :])
                ins.then_inc(x1T_psum, 1)

            def logits(t):
                pe.wait_ge(x1T_act, t + 1)
                for k in range(KD):
                    if k == 4:
                        pe.wait_ge(x1T_dve, t + 1)
                    ins = pe.matmul(bank[6 + t][:, 0:NE], x1T[:, k, t * P:(t + 1) * P], w_router[:, k, :],
                                    start=(k == 0), stop=(k == KD - 1))
                ins.then_inc(logit_psum, 1)

            pe.wait_ge(w_out_full[0], 16)
            pe.wait_ge(w_out_full[1], 16)
            pe.wait_ge(att_ready, 2)
            pe.wait_ge(probT_ready, 6)
            mix(0, 4)
            pe.wait_ge(gla_normed, 2)
            for h in range(GH):
                for t in range(T):
                    ins = pe.transpose(bank[4 + h // 2][:, (h % 2) * S + t * P:(h % 2) * S + (t + 1) * P],
                                       gla_o[:, t, h * GDV:(h + 1) * GDV], ident[:, :])
                if h % 2:
                    ins.then_inc(glaT_psum, 1)
            mix(1, 4)
            pe.wait_ge(glaT_ready, 2)
            mix(0, 0)
            mix(1, 0, (0,))
            turn_x1(0, 0)
            turn_x1(0, 1)
            mix(1, 0, (1,))
            turn_x1(1, 0)
            pe.wait_ge(router_scaled, 1)
            logits(0)
            turn_x1(1, 1)
            logits(1)
            pe.wait_ge(mask_ready, 2)
            pe.matmul(bank[5][0:1, 0:NE], ones[:, 0:1], mask[:, 0, :], start=True, stop=False)
            pe.matmul(bank[5][0:1, 0:NE], ones[:, 0:1], mask[:, 1, :], start=False, stop=True)
            pe.matmul(bank[4][:, 0:NE], before[:, :], mask[:, 0, :], start=True, stop=True)
            pe.matmul(bank[4][:, NE:2 * NE], ones[:, :], mask[:, 0, :], start=True, stop=False)
            pe.matmul(bank[4][:, NE:2 * NE], before[:, :], mask[:, 1, :], start=False, stop=True).then_inc(rank_psum, 1)

            def pack(j, a, first, halves=(0, 1)):
                pe.wait_ge(route_ready, j + 1)
                if first:
                    pe.wait_ge(h2_ready, 2)
                elif a == 0:
                    pe.wait_ge(comb_added, 4 * j)
                for c in range(4 * halves[0], 4 * halves[-1] + 4):
                    for t in range(T):
                        for i in range(3):
                            ins = pe.matmul(bank[6 + c // 4][:, (c % 4) * P:(c % 4 + 1) * P],
                                            h2_parts[i][:, t, c * P:(c + 1) * P], pick[a][:, t, :],
                                            start=(t == 0 and i == 0), stop=(t == T - 1 and i == 2))
                            if a == 1 and c == 0 and t == 0 and i == 0:
                                ins.then_inc(chunks_used, 1)
                    if c % 4 == 3:
                        ins.then_inc(pack_psum, 1)

            def chunk(c, first):
                return extra[c - FIRST_EXTRA] if first and FIRST_EXTRA <= c < RING else ring[:, c % RING, :]

            def arrived(it, c, first):
                if first and FIRST_EXTRA <= c < RING:
                    pe.wait_ge(extra_full[c - FIRST_EXTRA], 16)
                    return
                fills = c // RING + (1 if c % RING < FIRST_EXTRA else 0)
                pe.wait_ge(ring_full[c % RING], it * (16 * (ITER_CHUNKS // RING)) + 16 * fills)

            def hidden_bias(j, a, first):
                pe.wait_ge(bias_pick_ready, j + 1)
                if first:
                    pe.wait_ge(bias_split, 1)
                    pe.wait_ge(x1_ready, 4)
                    pe.wait_ge(x1T_act, 1)
                    pe.wait_ge(x1T_dve, 1)
                else:
                    pe.wait_ge(hidden_ready, 2 * j)
                    pe.wait_ge(gatherT_ready, j)
                for n in range(4):
                    pe.matmul(bank[n][:, :], bias_pick[a], bias_parts[:, n * GROUP:(n + 1) * GROUP],
                              start=True, stop=False, skip_group_check=True)

            def up(it, j, a, first):
                hidden_bias(j, a, first)
                if first:
                    pack(j, 0, True, (0,))
                for k in range(KD):
                    if first and k == KD // 2:
                        pack(j, 0, True, (1,))
                    if k % (KD // 2) == 0:
                        pe.wait_ge(pack_ready, 2 * j + 1 + 2 * k // KD)
                    c = a * JOB_CHUNKS + 2 * k
                    arrived(it, c, first)
                    arrived(it, c + 1, first)
                    for n in (0, 2, 1, 3):
                        for e in range(2):
                            ins = pe.matmul(bank[n][64 * e:64 * e + 64, :], xeT[a][:, k, 64 * e:64 * e + 64],
                                            chunk(c + e, first)[:, n * GROUP:(n + 1) * GROUP],
                                            start=False, stop=(k == KD - 1), skip_group_check=True)
                            if n == 3 and (e == 0 or k < KD - 1):
                                ins.then_inc(chunks_used, 1)
                        if k == KD - 1:
                            ins.then_inc(hidden_psum, 1)

            def turn(j, a, first):
                if not first:
                    pe.wait_ge(comb_added, 4 * j)
                for hf in range(2):
                    pe.wait_ge(hidden_ready, 2 * j + hf + 1)
                    for i in range(4):
                        ins = pe.transpose(bank[4 + hf][:, i * P:(i + 1) * P], act_t[:, hf, i * P:(i + 1) * P], ident[:, :])
                        if a == 1 and hf == 0 and i == 0:
                            ins.then_inc(chunks_used, 1)
                    ins.then_inc(hiddenT_psum, 1)
                pe.wait_ge(gated_ready, j + 1)
                for t in range(T):
                    ins = pe.transpose(bank[0][:, t * P:(t + 1) * P], pick_gated[a][:, t, :], ident[:, :])
                ins.then_inc(gatherT_psum, 1)

            def down(it, j, a, first):
                pe.wait_ge(pack_ready, 2 * j + 4 if a == 0 else 2 * j + 2)
                pe.wait_ge(hiddenT_ready, 2 * j + 2)
                for dh in range(2):
                    c0 = 2 * D + dh * GROUP
                    pe.matmul(bank[6 + dh][:, :], bias_pick[a], bias_parts[:, c0:c0 + GROUP],
                              start=True, stop=False, skip_group_check=True)
                for k in range(KD):
                    c = a * JOB_CHUNKS + 2 * KD + k
                    arrived(it, c, False)
                    for dh in range(2):
                        for e in range(2):
                            f = e * D + dh * GROUP
                            ins = pe.matmul(bank[6 + dh][64 * e:64 * e + 64, :], actT[:, k, 64 * e:64 * e + 64],
                                            ring[:, c % RING, f:f + GROUP], start=False, stop=(k == KD - 1),
                                            skip_group_check=True)
                        if k == KD - 1:
                            ins.then_inc(y_psum, 1)
                        elif dh == 1:
                            ins.then_inc(chunks_used, 1)

            def spread(j):
                pe.wait_ge(gatherT_ready, j + 1)
                for n in range(4):
                    dh, t = divmod(n, 2)
                    pe.wait_ge(y_ready, 2 * j + 1 + dh)
                    ins = pe.matmul(bank[4 + n][:, :], gatherT[:, t * P:(t + 1) * P], y_sb[:, dh, :],
                                    start=True, stop=True)
                    ins.then_inc(comb_psum if n else chunks_used, 1)

            def run(it, quad, rnd):
                first = isinstance(it, int)
                j = it * PAIRS
                if not first:
                    pack(j, 0, False)
                up(it, j, 0, first)
                pack(j + 1, 1, False)
                turn(j, 0, first)
                down(it, j, 0, first)
                spread(j)
                up(it, j + 1, 1, False)
                turn(j + 1, 1, False)
                down(it, j + 1, 1, False)
                spread(j + 1)

            all_rounds(pe, run)


_INS = ['x', 'norm1_g', 'w_in', 'gla_gate_up', 'gla_gate_bias', 'gla_norm_g', 'q_norm_g', 'k_norm_g',
        'rel_bias', 'w_out', 'norm2_g', 'router_w', 'router_b', 'moe_w_in', 'moe_b_in', 'moe_w_out', 'moe_b_out']
_OUTS = [((1, S, D), 'float32')]


def kernel(**inputs):
    import numpy as _np
    import concourse.bacc as _bacc
    from concourse import mybir as _mybir
    from concourse.bass_utils import run_bass_kernel_spmd as _run

    nc = _bacc.Bacc("TRN2", target_bir_lowering=False, num_devices=1)
    arrays, args = {}, []
    for name in _INS:
        a = _np.ascontiguousarray(inputs[name])
        arrays[f"in_{name}_dram"] = a
        args.append(nc.dram_tensor(f"in_{name}_dram", a.shape, _mybir.dt.from_np(a.dtype), kind="ExternalInput").ap())
    for i, (shape, dtype) in enumerate(_OUTS):
        dt = _mybir.dt.from_np(_np.dtype(dtype))
        args.append(nc.dram_tensor(f"out_{i}_dram", shape, dt, kind="ExternalOutput").ap())
    build(nc, *args)
    r = _run(nc, [arrays], core_ids=[0])
    return r.results[0]["out_0_dram"]
```
